# Optimizing a Trainium2 kernel written in Bass

```python
import math
import jax, jax.numpy as jnp
from jax import lax
import numpy as np

D_MODEL = 2048
BATCH = 1
SEQ = 256
DEPTH = 2

HEAD_DIM = 128
N_HEADS = 8
N_KV_HEADS = 2
IDX_HEADS = 16
IDX_DIM = 64
MAX_TOPK = 256
Q_BLOCK = 128
CONV_CH = 512
CONV_WIDTH = 31
MEM_LEN = 256
MEM_HEADS = 4
FFN_DIM = 4 * D_MODEL
ROPE_THETA = 500000.0
ROT_FRACTION = 4
N_BRANCH = 3
EPS = 1e-6

ATTN_DIM = N_HEADS * HEAD_DIM
KV_DIM = N_KV_HEADS * HEAD_DIM
MEM_DIM = MEM_HEADS * HEAD_DIM
SPLITS = (ATTN_DIM, KV_DIM, KV_DIM, IDX_HEADS * IDX_DIM, IDX_DIM, IDX_HEADS,
          2 * CONV_CH, MEM_DIM, N_BRANCH * D_MODEL)
N_IN = sum(SPLITS)

kernel_name = "hybrid_dsa_conformer_memory_gated_block"

def rms_norm(x, g):
    xf = x.astype(jnp.float32)
    y = xf * lax.rsqrt(jnp.mean(xf * xf, axis=-1, keepdims=True) + EPS)
    return (y * g.astype(jnp.float32)).astype(x.dtype)

def layer_norm(x, g, b):
    xf = x.astype(jnp.float32)
    mu = jnp.mean(xf, axis=-1, keepdims=True)
    var = jnp.mean(jnp.square(xf - mu), axis=-1, keepdims=True)
    y = (xf - mu) * lax.rsqrt(var + EPS)
    return (y * g.astype(jnp.float32) + b.astype(jnp.float32)).astype(x.dtype)

def rope_tables(positions, rot_dim):
    half = rot_dim // 2
    inv_freq = ROPE_THETA ** (-jnp.arange(half, dtype=jnp.float32) * 2.0 / rot_dim)
    ang = positions.astype(jnp.float32)[..., None] * inv_freq
    return jnp.cos(ang)[:, :, None, :], jnp.sin(ang)[:, :, None, :]

def apply_partial_rope(t, cos, sin):
    half = cos.shape[-1]
    rot = 2 * half
    tf = t.astype(jnp.float32)
    t1, t2, tp = tf[..., :half], tf[..., half:rot], tf[..., rot:]
    out = jnp.concatenate([t1 * cos - t2 * sin, t2 * cos + t1 * sin, tp], axis=-1)
    return out.astype(t.dtype)

def dsa_sparse_attention(q, k, v, iq, ik, iw):
    B, S = q.shape[0], q.shape[1]
    topk = min(MAX_TOPK, S // 4)
    nb = S // Q_BLOCK
    group = N_HEADS // N_KV_HEADS
    scale = HEAD_DIM ** -0.5
    idx_scale = (IDX_DIM ** -0.5) * (IDX_HEADS ** -0.5)
    key_pos = jnp.arange(S, dtype=jnp.int32)
    starts = jnp.arange(nb, dtype=jnp.int32) * Q_BLOCK
    gather = jax.vmap(lambda t, i: t[i])

    def to_blocks(t):
        return t.reshape((B, nb, Q_BLOCK) + t.shape[2:]).swapaxes(0, 1)

    def block(args):
        qb, iqb, iwb, t0 = args
        s_idx = jnp.einsum('bqhd,bsd->bqhs', iqb, ik).astype(jnp.float32)
        index = jnp.einsum('bqh,bqhs->bqs', iwb.astype(jnp.float32),
                           jax.nn.relu(s_idx)) * idx_scale
        q_pos = t0 + jnp.arange(Q_BLOCK, dtype=jnp.int32)
        causal = key_pos[None, :] <= q_pos[:, None]
        index = jnp.where(causal[None], index, -jnp.inf)
        sel_val, sel_idx = lax.top_k(index, topk)
        valid = jnp.isfinite(sel_val)
        k_sel = gather(k, sel_idx)
        v_sel = gather(v, sel_idx)
        qg = qb.reshape(B, Q_BLOCK, N_KV_HEADS, group, HEAD_DIM)
        logits = jnp.einsum('bqkgd,bqnkd->bqkgn', qg, k_sel).astype(jnp.float32) * scale
        logits = jnp.where(valid[:, :, None, None, :], logits, -jnp.inf)
        p = jax.nn.softmax(logits, axis=-1).astype(v.dtype)
        o = jnp.einsum('bqkgn,bqnkd->bqkgd', p, v_sel)
        return o.reshape(B, Q_BLOCK, N_HEADS * HEAD_DIM)

    out = lax.map(block, (to_blocks(q), to_blocks(iq), to_blocks(iw), starts))
    return out.swapaxes(0, 1).reshape(B, S, N_HEADS * HEAD_DIM)

def memory_cross_attention(q, mk, mv):
    B, S = q.shape[0], q.shape[1]
    logits = jnp.einsum('bshd,bmhd->bhsm', q, mk).astype(jnp.float32) * (HEAD_DIM ** -0.5)
    p = jax.nn.softmax(logits, axis=-1).astype(mv.dtype)
    o = jnp.einsum('bhsm,bmhd->bshd', p, mv)
    return o.reshape(B, S, MEM_HEADS * HEAD_DIM)

def conformer_conv(glu_in, conv_in_b, conv_w, conv_b, ln_g, ln_b):
    a, gte = jnp.split(glu_in + conv_in_b, 2, axis=-1)
    u = a * jax.nn.sigmoid(gte)
    y = lax.conv_general_dilated(
        u, conv_w[:, None, :].astype(u.dtype), window_strides=(1,),
        padding=[(CONV_WIDTH - 1, 0)],
        dimension_numbers=('NWC', 'WIO', 'NWC'),
        feature_group_count=CONV_CH) + conv_b
    y = layer_norm(y, ln_g, ln_b)
    return jax.nn.silu(y)

def setup_inputs(seed: int = 0) -> dict:
    key = jax.random.key(seed)
    ks = jax.random.split(key, 32)

    def nrm(k, shape, fan_in, extra=1.0):
        return jax.random.normal(k, shape, jnp.float32) * (fan_in ** -0.5) * extra

    def gain(k, shape):
        return 1.0 + 0.1 * jax.random.normal(k, shape, jnp.float32)

    def bias(k, shape):
        return 0.02 * jax.random.normal(k, shape, jnp.float32)

    res_scale = (2 * DEPTH) ** -0.5
    x = jax.random.normal(ks[0], (BATCH, SEQ, D_MODEL), jnp.float32)
    mem = jax.random.normal(ks[1], (BATCH, MEM_LEN, D_MODEL), jnp.float32)
    offsets = jax.random.randint(ks[2], (BATCH, 1), 0, 1024, dtype=jnp.int32)
    positions = offsets + jnp.arange(SEQ, dtype=jnp.int32)[None, :]
    return {
        "x": x,
        "mem": mem,
        "positions": positions,
        "norm1_g": gain(ks[3], (DEPTH, D_MODEL)),
        "w_in": nrm(ks[4], (DEPTH, D_MODEL, N_IN), D_MODEL),
        "q_norm_g": gain(ks[5], (DEPTH, HEAD_DIM)),
        "k_norm_g": gain(ks[6], (DEPTH, HEAD_DIM)),
        "mem_norm_g": gain(ks[7], (DEPTH, D_MODEL)),
        "w_mem_kv": nrm(ks[8], (DEPTH, D_MODEL, 2 * MEM_DIM), D_MODEL),
        "mq_norm_g": gain(ks[9], (DEPTH, HEAD_DIM)),
        "mk_norm_g": gain(ks[10], (DEPTH, HEAD_DIM)),
        "conv_in_b": bias(ks[11], (DEPTH, 2 * CONV_CH)),
        "conv_w": nrm(ks[12], (DEPTH, CONV_WIDTH, CONV_CH), CONV_WIDTH),
        "conv_b": bias(ks[13], (DEPTH, CONV_CH)),
        "conv_ln_g": gain(ks[14], (DEPTH, CONV_CH)),
        "conv_ln_b": bias(ks[15], (DEPTH, CONV_CH)),
        "gate_b": bias(ks[16], (DEPTH, N_BRANCH * D_MODEL)),
        "w_attn_o": nrm(ks[17], (DEPTH, ATTN_DIM, D_MODEL), ATTN_DIM),
        "w_mem_o": nrm(ks[18], (DEPTH, MEM_DIM, D_MODEL), MEM_DIM),
        "w_conv_o": nrm(ks[19], (DEPTH, CONV_CH, D_MODEL), CONV_CH),
        "conv_o_b": bias(ks[20], (DEPTH, D_MODEL)),
        "w_out": nrm(ks[21], (DEPTH, D_MODEL, D_MODEL), D_MODEL, res_scale),
        "norm2_g": gain(ks[22], (DEPTH, D_MODEL)),
        "w_up": nrm(ks[23], (DEPTH, D_MODEL, FFN_DIM), D_MODEL),
        "w_down": nrm(ks[24], (DEPTH, FFN_DIM, D_MODEL), FFN_DIM, res_scale),
    }

def reference(x, mem, positions, norm1_g, w_in, q_norm_g, k_norm_g, mem_norm_g,
              w_mem_kv, mq_norm_g, mk_norm_g, conv_in_b, conv_w, conv_b,
              conv_ln_g, conv_ln_b, gate_b, w_attn_o, w_mem_o, w_conv_o,
              conv_o_b, w_out, norm2_g, w_up, w_down):
    B, S, _ = x.shape
    M = mem.shape[1]
    cos_h, sin_h = rope_tables(positions, HEAD_DIM // ROT_FRACTION)
    cos_i, sin_i = rope_tables(positions, IDX_DIM // ROT_FRACTION)
    bounds = np.cumsum(SPLITS)[:-1].tolist()

    for l in range(DEPTH):
        h = rms_norm(x, norm1_g[l])
        proj = h @ w_in[l]
        q, k, v, iq, ik, iw, glu_in, mq, gates = jnp.split(proj, bounds, axis=-1)

        q = apply_partial_rope(rms_norm(q.reshape(B, S, N_HEADS, HEAD_DIM), q_norm_g[l]), cos_h, sin_h)
        k = apply_partial_rope(rms_norm(k.reshape(B, S, N_KV_HEADS, HEAD_DIM), k_norm_g[l]), cos_h, sin_h)
        v = v.reshape(B, S, N_KV_HEADS, HEAD_DIM)
        iq = apply_partial_rope(iq.reshape(B, S, IDX_HEADS, IDX_DIM), cos_i, sin_i)
        ik = apply_partial_rope(ik[:, :, None, :], cos_i, sin_i)[:, :, 0, :]
        y_attn = dsa_sparse_attention(q, k, v, iq, ik, iw) @ w_attn_o[l]

        m = rms_norm(mem, mem_norm_g[l])
        mkv = (m @ w_mem_kv[l]).reshape(B, M, 2, MEM_HEADS, HEAD_DIM)
        mk = rms_norm(mkv[:, :, 0], mk_norm_g[l])
        mv = mkv[:, :, 1]
        mq = rms_norm(mq.reshape(B, S, MEM_HEADS, HEAD_DIM), mq_norm_g[l])
        y_mem = memory_cross_attention(mq, mk, mv) @ w_mem_o[l]

        y_conv = conformer_conv(glu_in, conv_in_b[l], conv_w[l], conv_b[l],
                                conv_ln_g[l], conv_ln_b[l]) @ w_conv_o[l] + conv_o_b[l]

        g = jax.nn.sigmoid(gates + gate_b[l]).reshape(B, S, N_BRANCH, D_MODEL)
        merged = g[:, :, 0] * y_attn + g[:, :, 1] * y_mem + g[:, :, 2] * y_conv
        x = x + merged @ w_out[l]

        h2 = rms_norm(x, norm2_g[l])
        x = x + jnp.square(jax.nn.relu(h2 @ w_up[l])) @ w_down[l]
    return x


_drawn_inputs = setup_inputs


def setup_inputs(seed=0):
    import zlib

    import numpy as np

    out = dict(_drawn_inputs(seed))
    spreads = {}
    factors = {'q_norm_g': 6.547,
     'k_norm_g': 6.44,
     'mem_norm_g': 8.0,
     'mq_norm_g': 8.0,
     'mk_norm_g': 8.0,
     'conv_in_b': 8.0,
     'conv_b': 5.302,
     'conv_ln_b': 8.0,
     'gate_b': 8.0,
     'conv_o_b': 7.017}
    for name, (base, spread) in spreads.items():
        noise = np.random.default_rng([zlib.crc32(name.encode()), seed]).standard_normal(out[name].shape)
        drawn = base * np.exp(spread * noise) if base else spread * noise
        out[name] = __import__('jax').numpy.asarray(drawn.astype(out[name].dtype))
    for name, factor in factors.items():
        out[name] = (out[name] * factor).astype(out[name].dtype)
    return out
```

```python
from contextlib import ExitStack, contextmanager

import numpy as np

import concourse.bass as bass
from concourse import mybir

F32 = mybir.dt.float32
F32R = mybir.dt.float32r
I32 = mybir.dt.int32
ALU = mybir.AluOpType
ACT = mybir.ActivationFunctionType
AX_X = mybir.AxisListType.X

P = 128
LAYERS = 2
SEQ = 256
T = SEQ // P
D = 2048
KT = D // P
HEAD = 128
HEADS, KV_HEADS, MEM_HEADS = 8, 2, 4
IDX_HEADS, IDX_DIM = 16, 64
TOPK = 64
CONV = 512
TAPS = 31
FFN = 4 * D
EPS = 1e-6
COL = 512
CB = D // COL
SCALE = float(HEAD) ** -0.5
IDX_SCALE = float(IDX_DIM) ** -0.5 * float(IDX_HEADS) ** -0.5

Q0 = 0
K0 = Q0 + HEADS * HEAD
V0 = K0 + KV_HEADS * HEAD
IQ0 = V0 + KV_HEADS * HEAD
IK0 = IQ0 + IDX_HEADS * IDX_DIM
IW0 = IK0 + IDX_DIM
GLU0 = IW0 + IDX_HEADS
MQ0 = GLU0 + 2 * CONV
GATE0 = MQ0 + MEM_HEADS * HEAD
IKW = IDX_DIM + IDX_HEADS

FRONT = 11
UNITS = 8
CHUNKS = 4
(G_IKW, G_IQ0, G_IQ1, G_GLUA, G_GLUG, G_MK, G_MV, G_MQ, G_KV, G_Q0, G_Q1) = range(FRONT)
GROUPS = FRONT + 4 * CB + CB + 2 * FFN // COL

HALF_A, HALF_I = HEAD // 4 // 2, IDX_DIM // 4 // 2
THETA = 500000.0
TWO_PI = 6.283185307179586
PI_1 = 6.28125
PI_2 = 0.0019340515136718750
PI_3 = TWO_PI - PI_1 - PI_2
ROUND = 1.5 * 2.0 ** 23
PI_MAX = 3.1415925

UNSEEN = -(2.0 ** 127)
TAKEN = -1.5 * 2.0 ** 127
BIG = 1e30

MEM_FILL = [[8, 9, 10, 11], [18, 19, 20, 21]]
TAPS_FILL = 2
IK_FILL = 14
IQ_FILL = [[22, 23], [29, 30]]
INDEX_AT = 36
CONV_IN_FILL = [50, 51]
MK_FILL = [57, 58]
MQ_FILL = [73, 74]
K_FILL = [81, 82]
Q_FILL = [[86, 87], [94, 95]]
CONV_OUT_FILL = [88, 89]
CONV_ROW_FILL = [104, 105]
HEAD_AT = [79 + 2 * j for j in range(4)] + [90 + 2 * j for j in range(8)]
CONV_AT, CONV_STEPS = 56, 4
TOPK_AT = 58


def front_fills():
    f = [(TAPS_FILL, "taps", 0, 0), (IK_FILL, "ik", 0, 0)]
    f += [(n, "k", h, 0) for h, n in enumerate(K_FILL)]
    f += [(MEM_FILL[t][i], "mem", t, i) for t in range(T) for i in range(KT // 4)]
    f += [(IQ_FILL[h][t], "iq", h, t) for h in range(2) for t in range(T)]
    f += [(n, "conv_in", t, 0) for t, n in enumerate(CONV_IN_FILL)]
    f += [(n, "mk", t, 0) for t, n in enumerate(MK_FILL)]
    f += [(n, "mq", t, 0) for t, n in enumerate(MQ_FILL)]
    f += [(Q_FILL[h][t], "q", h, t) for h in range(2) for t in range(T)]
    f += [(n, "conv_out", t, 0) for t, n in enumerate(CONV_OUT_FILL)]
    f += [(n, "conv_row", t, 0) for t, n in enumerate(CONV_ROW_FILL)]
    f += [(b + 5, "p", j, 0) for j, b in enumerate(HEAD_AT)]
    f += [(b + 7, "o", j, 0) for j, b in enumerate(HEAD_AT)]
    return sorted(f)


FILLS = front_fills()
NORM_FILLS = T * KT // 4
EMPTY_AFTER = 4


def fills_until(name):
    return NORM_FILLS + [f[1:] for f in FILLS].index(name) + 1


IKW_TAKEN, IQ_TAKEN = 11, [19, 27]
MEM_SQUARES, MEM_MEAN, MEM_NORM = [5, 17], [6, 18], [7, 19]
GLU_A_TAKEN, GLU_G_TAKEN, GLU_EXP = 36, 44, 45
ROWS_TAKEN = [52, 68, 76, 84, 92]
MV_TAKEN = 60
MASK_FREE = 60
LN_STATS, LN_APPLY, Y_EXP = 94, 96, 99
GATE_TAKEN, GATE_EXP = [12, 20, 28], [13, 21, 29]
BIAS_AT = 8
FRONT_DMAS = 7
FREQ_A = [float(np.float32(THETA) ** (np.float32(-2.0 * i) / np.float32(2 * HALF_A))) for i in range(HALF_A)]
FREQ_I = [float(np.float32(THETA) ** (np.float32(-2.0 * i) / np.float32(2 * HALF_I))) for i in range(HALF_I)]

PER = {
    "layer": {"group": GROUPS, "unit": GROUPS * UNITS, "acc0": 36, "acc1": 35, "fill": 110, "tp0": 55, "tp1": 55,
              "tp_hi": 78, "score": 28, "sc0": 14, "sc1": 14, "squared": 48, "x_new": 20,
              "dve_step": 203, "pool_step": 46, "gain_in": 48, "mem_in": 32, "front_in": 16 * FRONT_DMAS,
              "ln_in": 32, "bias_in": 32 * CB, "parked": 32, "x_back": 16, "mean_ready": 6, "rstd_ready": 6,
              "normed": 6, "ik_turned": 1, "iq_turned": 2, "relu_used": IDX_HEADS, "causal_done": 2, "chosen": 1,
              "glu_here": 1, "glu_exp": 1, "glu_done": 1, "pad_ready": 1, "conv_done": 1, "ln_stat": 1,
              "ln_root": 1, "ln_done": 1, "ln_scaled": 1, "y_exp": 1, "swish_done": 1, "rows_here": 5,
              "head_mean": 5, "rows_ready": 5, "logits": 12, "exps": 12, "inv_ready": 12, "probs": 12,
              "gate_in": 12, "gate_exp": 12, "gate_one": 12, "bias_used": CB, "merged_ready": CB,
              "hid_relu": 16, "hid_ready": 16},
    "merge": {"group": 4, "unit": 32, "acc0": 3, "acc1": 3, "fill": 2, "tp0": 1, "tp1": 1, "tp_hi": 2,
              "dve_step": 7, "bias_in": 32, "gate_in": 3, "gate_exp": 3, "gate_one": 3, "bias_used": 1,
              "merged_ready": 1},
    "ffn": {"group": 8, "unit": 64, "acc0": 4, "acc1": 4, "fill": 8, "tp0": 4, "tp1": 4, "tp_hi": 8,
            "squared": 8, "x_new": 4, "hid_relu": 4, "hid_ready": 4},
}


class Place:

    def __init__(self, names):
        self.base = dict.fromkeys(names, 0)
        self.n = dict.fromkeys(names, 0)
        self.bank = 0
        self.mark = {}
        self.counted = set()

    def now(self, name):
        return self.base[name] + self.n[name]

    def next(self, name, by=1):
        self.n[name] += by
        self.counted.add(name)
        return self.now(name)

    def fill(self, name):
        b = self.bank
        self.bank = 1 - b
        self.next(f"tp{b}")
        self.mark[name] = (b, self.n[f"tp{b}"])
        return b

    def emptied(self, name):
        b, k = self.mark[name]
        return b, self.base[f"tp{b}"] + k + 1

    @contextmanager
    def loop(self, kind, i, first, trips):
        base, n, bank = dict(self.base), dict(self.n), self.bank
        for name in self.base:
            per = PER[kind].get(name, 0)
            self.base[name] = base[name] + n[name] + (i - first) * per
            self.n[name] = 0
        yield
        assert self.bank == bank, kind
        for name in self.base:
            per = PER[kind].get(name, 0)
            assert name not in self.counted or self.n[name] == per, (kind, name, self.n[name])
            self.base[name] = base[name]
            self.n[name] = n[name] + trips * per


def build(nc, x, mem, positions, norm1_g, w_in, q_norm_g, k_norm_g, mem_norm_g, w_mem_kv, mq_norm_g,
          mk_norm_g, conv_in_b, conv_w, conv_b, conv_ln_g, conv_ln_b, gate_b, w_attn_o, w_mem_o,
          w_conv_o, conv_o_b, w_out, norm2_g, w_up, w_down, out):
    ctx = ExitStack()
    with ctx:
        kb = 1024
        base = (nc.sbuf_base + 31) // 32 * 32
        ctx.enter_context(nc.sbuf_tensor("arena", [P, nc.sbuf_usable_end - base - 64], mybir.dt.uint8))

        def at(name, shape, offset, dt=F32):
            n = 4
            for s in shape[1:]:
                n *= s
            assert base + offset + n <= nc.sbuf_usable_end, name
            return nc.alloc_sbuf_tensor_at(name, shape, dt, offset=base + int(offset))

        raw = at("raw", [P, CHUNKS, 4, COL], 0)
        hi = at("hi", [P, 4, 2, COL], 32 * kb, F32R)
        lo = at("lo", [P, 4, 2, COL], 48 * kb, F32R)
        hT_hi = at("hT_hi", [P, KT, SEQ], 64 * kb, F32R)
        hT_lo = at("hT_lo", [P, KT, SEQ], 80 * kb, F32R)
        bT_hi = at("bT_hi", [P, KT, SEQ], 96 * kb, F32R)
        bT_lo = at("bT_lo", [P, KT, SEQ], 112 * kb, F32R)
        B = 96 * kb
        mqT = at("mqT", [P, MEM_HEADS, SEQ], B)
        q_tok = at("q_tok", [P, T, HEADS, HEAD], B + 4 * kb)
        qT = at("qT", [P, HEADS, SEQ], B + 12 * kb)
        kv_tok = at("kv_tok", [P, T, 2 * KV_HEADS, HEAD], B + 20 * kb)
        kT = at("kT", [P, KV_HEADS, SEQ], B + 24 * kb)
        s_buf = at("s_buf", [P, 3, T, SEQ], B + 26 * kb)
        X = 128 * kb
        x_tok = at("x_tok", [P, T, D], X)
        iq_tok = at("iq_tok", [P, T, IDX_HEADS, IDX_DIM], X)
        iqT = at("iqT", [P, IDX_HEADS // 2, SEQ], X + 8 * kb)
        mask = at("mask", [P, T, SEQ], X)
        ln_g = at("ln_g", [P, CONV], X + 2 * kb)
        ln_b = at("ln_b", [P, CONV], X + 4 * kb)
        y_tok = at("y_tok", [P, T, CONV], X + 6 * kb)
        y_sig = at("y_sig", [P, T, CONV], X + 12 * kb)
        S = 144 * kb
        W = S + 6 * kb
        wide = at("wide", [P, D], W)
        gain = at("gain", [P, D], W + 8 * kb)
        mk_tok = at("mk_tok", [P, T, MEM_HEADS, HEAD], W)
        mkT = at("mkT", [P, MEM_HEADS, SEQ], W + 4 * kb)
        mv_tok = at("mv_tok", [P, T, MEM_HEADS, HEAD], W + 8 * kb)
        mq_tok = at("mq_tok", [P, T, MEM_HEADS, HEAD], W + 12 * kb)
        pT = at("pT", [P, 2, T, SEQ], W + 12 * kb)
        gates = at("gates", [P, 3, T, COL], W)
        merged = at("merged", [P, T, COL], W + 12 * kb)
        cT_hi = at("cT_hi", [P, CONV // P, SEQ], S + 22 * kb, F32R)
        cT_lo = at("cT_lo", [P, CONV // P, SEQ], S + 26 * kb, F32R)
        oT_hi = at("oT_hi", [P, HEADS, SEQ], S + 30 * kb, F32R)
        oT_lo = at("oT_lo", [P, HEADS, SEQ], S + 38 * kb, F32R)
        moT_hi = at("moT_hi", [P, MEM_HEADS, SEQ], S + 46 * kb, F32R)
        moT_lo = at("moT_lo", [P, MEM_HEADS, SEQ], S + 50 * kb, F32R)
        relu = at("relu", [P, 2, T, SEQ], S + 22 * kb)
        index = at("index", [P, T, SEQ], S + 26 * kb)
        hidden = at("hidden", [P, 2, T, COL], S + 22 * kb)
        glu_a = at("glu_a", [P, T, CONV], S + 30 * kb)
        glu_g = at("glu_g", [P, T, CONV], S + 34 * kb)
        uT = at("uT", [P, CONV // P, TAPS - 1 + SEQ], S + 38 * kb)
        conv_acc = at("conv_acc", [P, CONV // P, SEQ], S + 54 * kb)
        glu_b = at("glu_b", [P, 2, CONV], S + 54 * kb)
        squares = at("squares", [P, T, COL], S + 58 * kb)
        tap_rows = at("tap_rows", [TAPS + 1, CONV], S + 58 * kb)
        ikw_tok = at("ikw_tok", [P, T, IKW], S + 60 * kb)
        ik_twice = at("ik_twice", [P, T, 2, IDX_DIM], S + 61 * kb)
        gate_bias = at("gate_bias", [P, 3, COL], S + 54 * kb)
        conv_bias = at("conv_bias", [P, COL], S + 60 * kb)
        rope_tmp = at("rope_tmp", [P, 2, P], S + 62 * kb)
        tapT = at("tapT", [P, CONV // P, TAPS + 1], S + 63 * kb)
        small = [S]

        def keep(name, shape, dt=F32):
            tensor = at(name, shape, small[0], dt)
            n = 4
            for s in shape[1:]:
                n *= s
            small[0] += (n + 31) // 32 * 32
            assert small[0] <= S + 6 * kb
            return tensor

        ident = keep("ident", [P, P])
        ikT = keep("ikT", [P, SEQ])
        head_gain = keep("head_gain", [P, 4, HEAD])
        NF = HALF_A + HALF_I
        pos_i = keep("pos_i", [P, T], I32)
        pos_f = keep("pos_f", [P, T])
        freq = keep("freq", [P, NF])
        turns = keep("turns", [P, T, NF])
        angle = keep("angle", [P, T, NF])
        fold = keep("fold", [P, T, NF])
        sin = keep("sin", [P, T, NF])
        cos = keep("cos", [P, T, NF])
        half_pi = keep("half_pi", [P, 1])
        minus_half = keep("minus_half", [P, 8])
        sq_sum = keep("sq_sum", [P, T, CB])
        mem_sum = keep("mem_sum", [P, T, CB])
        mean_sq = keep("mean_sq", [P, T])
        rstd = keep("rstd", [P, T])
        head_sum = keep("head_sum", [P, 8])
        head_rstd = keep("head_rstd", [P, 8])
        iw = keep("iw", [P, T, IDX_HEADS])
        top8 = keep("top8", [P, T, 8])
        neg_max = keep("neg_max", [P, 3, T])
        p_sum = keep("p_sum", [P, 3, T])
        p_inv = keep("p_inv", [P, 3, T])
        bn = keep("bn", [P, T, 6])
        mean_var = keep("mean_var", [P, T, 2])
        ln_rstd = keep("ln_rstd", [P, T])

        ROWS = [(G_MK, mk_tok[:, :, :, :], MEM_HEADS), (G_MQ, mq_tok[:, :, :, :], MEM_HEADS),
                (G_KV, kv_tok[:, :, :, :], KV_HEADS),
                (G_Q0, q_tok[:, :, 0:4], 4), (G_Q1, q_tok[:, :, 4:8], 4)]

        acc = ctx.enter_context(nc.psum_tensor("acc", [P, 2, T, COL], F32))
        tp = ctx.enter_context(nc.psum_tensor("tp", [P, 2, 4, P], F32))
        sc = ctx.enter_context(nc.psum_tensor("sc", [P, 2, T, SEQ], F32))

        x_park = nc.dram_tensor("x_park", (T, P, D), F32, kind="Internal").ap()

        def sem(name):
            return ctx.enter_context(nc.semaphore(name))

        landed = [sem(f"landed{c}") for c in range(CHUNKS)]
        hi_ready = sem("hi_ready")
        lo_ready = sem("lo_ready")
        unit_done = sem("unit_done")
        acc_free = [sem(f"acc_free{i}") for i in range(2)]
        tp_full = sem("tp_full")
        tp_free = [sem(f"tp_free{i}") for i in range(2)]
        tp_hi = sem("tp_hi")
        sc_full = sem("sc_full")
        sc_free = [sem(f"sc_free{i}") for i in range(2)]
        dve_step = sem("dve_step")
        act_step = sem("act_step")
        pool_step = sem("pool_step")
        ready = sem("ready")
        waited = sem("waited")
        x_in = sem("x_in")
        gain_in = sem("gain_in")
        mem_in = sem("mem_in")
        front_in = sem("front_in")
        ln_in = sem("ln_in")
        bias_in = sem("bias_in")
        parked = sem("parked")
        x_back = sem("x_back")
        out_done = sem("out_done")
        squared = sem("squared")
        mean_ready = sem("mean_ready")
        rstd_ready = sem("rstd_ready")
        normed = sem("normed")
        ik_turned = sem("ik_turned")
        iq_turned = sem("iq_turned")
        relu_ready = sem("relu_ready")
        relu_used = sem("relu_used")
        causal_done = sem("causal_done")
        chosen = sem("chosen")
        glu_here = sem("glu_here")
        glu_exp = sem("glu_exp")
        glu_done = sem("glu_done")
        pad_ready = sem("pad_ready")
        conv_done = sem("conv_done")
        ln_stat = sem("ln_stat")
        ln_root = sem("ln_root")
        ln_done = sem("ln_done")
        ln_scaled = sem("ln_scaled")
        y_exp = sem("y_exp")
        swish_done = sem("swish_done")
        rows_here = sem("rows_here")
        head_mean = sem("head_mean")
        rows_ready = sem("rows_ready")
        logits = sem("logits")
        exps = sem("exps")
        inv_ready = sem("inv_ready")
        probs = sem("probs")
        gate_in = sem("gate_in")
        gate_exp = sem("gate_exp")
        gate_one = sem("gate_one")
        bias_used = sem("bias_used")
        merged_ready = sem("merged_ready")
        x_new = sem("x_new")
        hid_relu = sem("hid_relu")
        hid_ready = sem("hid_ready")

        NAMES = ["group", "unit", "acc0", "acc1", "fill", "tp0", "tp1", "tp_hi", "score", "sc0", "sc1",
                 "dve_step", "act_step", "pool_step",
                 "gain_in", "mem_in", "front_in", "ln_in", "bias_in", "parked", "x_back", "squared",
                 "mean_ready", "rstd_ready", "normed", "ik_turned", "iq_turned",
                 "relu_ready", "relu_used", "causal_done", "chosen", "glu_here", "glu_exp", "glu_done",
                 "pad_ready", "conv_done", "ln_stat", "ln_root", "ln_done", "ln_scaled", "y_exp",
                 "swish_done", "rows_here", "head_mean", "rows_ready", "logits", "exps",
                 "inv_ready", "probs", "gate_in", "gate_exp", "gate_one", "bias_used", "merged_ready",
                 "x_new", "hid_relu", "hid_ready"]

        chunked = {"p": P, "k": 4}
        v_in = w_in.rearrange("l (c k p) n -> l c p k n", **chunked)
        v_mem = w_mem_kv.rearrange("l (c k p) n -> l c p k n", **chunked)
        v_ao = w_attn_o.rearrange("l (c k p) n -> l c p k n", **chunked)
        v_mo = w_mem_o.rearrange("l (c k p) n -> l c p k n", **chunked)
        v_co = w_conv_o.rearrange("l (c k p) n -> l c p k n", **chunked)
        v_out = w_out.rearrange("l (c k p) n -> l c p k n", **chunked)
        v_up = w_up.rearrange("l (c k p) n -> l c p k n", **chunked)
        v_down = w_down.rearrange("l (q c k p) n -> l q c p k n", c=CHUNKS, **chunked)
        v_gb = gate_b.rearrange("l (i n) -> l i n", i=3)
        tokens = x.rearrange("b (t p) d -> (b t) p d", p=P)
        mem_tokens = mem.rearrange("b (t p) d -> (b t) p d", p=P)
        out_tokens = out.rearrange("b (t p) d -> (b t) p d", p=P)

        def rows(row, parts=P):
            return row.partition_broadcast(parts)

        def over(ap, axis, n):
            shape = list(ap.shape)
            return ap.unsqueeze(axis).broadcast_to(shape[:axis] + [n] + shape[axis:])

        FRONT_SRC = {
            G_IKW: (v_in, IK0, IKW), G_IQ0: (v_in, IQ0, COL), G_IQ1: (v_in, IQ0 + COL, COL),
            G_GLUA: (v_in, GLU0, COL), G_GLUG: (v_in, GLU0 + CONV, COL), G_MK: (v_mem, 0, COL),
            G_MV: (v_mem, COL, COL), G_MQ: (v_in, MQ0, COL), G_KV: (v_in, K0, COL),
            G_Q0: (v_in, Q0, COL), G_Q1: (v_in, Q0 + COL, COL),
        }

        def width_of(g):
            return IKW if g == G_IKW else COL

        block = ctx.enter_context(nc.Block())

        @block.sync
        def _(sp):
            here = Place(["unit"])

            def load(c, source):
                sp.wait_ge(lo_ready, here.next("unit", 2))
                sp.sem_inc(waited, 1)
                sp.dma_start(raw[:, c, :, 0:source.shape[-1]], source).then_inc(landed[c], 16)

            with sp.Fori(0, LAYERS) as l, here.loop("layer", l, 0, LAYERS):
                for g in range(FRONT):
                    view, c0, w = FRONT_SRC[g]
                    for c in range(CHUNKS):
                        load(c, view[l, c, :, :, c0:c0 + w])
                with sp.Fori(0, CB) as cb, here.loop("merge", cb, 0, CB):
                    for i in range(3):
                        for c in range(CHUNKS):
                            load(c, v_in[l, c, :, :, bass.ds(GATE0 + i * D + cb * COL, COL)])
                    load(0, v_co[l, 0, :, :, bass.ds(cb * COL, COL)])
                    load(1, v_mo[l, 0, :, :, bass.ds(cb * COL, COL)])
                    load(2, v_ao[l, 0, :, :, bass.ds(cb * COL, COL)])
                    load(3, v_ao[l, 1, :, :, bass.ds(cb * COL, COL)])
                for b in range(CB):
                    for c in range(CHUNKS):
                        load(c, v_out[l, c, :, :, b * COL:(b + 1) * COL])
                with sp.Fori(0, FFN // D) as qu, here.loop("ffn", qu, 0, FFN // D):
                    for b in range(CB):
                        for c in range(CHUNKS):
                            load(c, v_up[l, c, :, :, bass.ds(qu * D + b * COL, COL)])
                    for b in range(CB):
                        for c in range(CHUNKS):
                            load(c, v_down[l, qu, c, :, :, b * COL:(b + 1) * COL])
            sp.wait_ge(x_new, LAYERS * (CB + CB * FFN // D))
            sp.dma_start(out_tokens.rearrange("t p d -> p t d"), x_tok[:, :, :]).then_inc(out_done, 16)
            sp.wait_ge(out_done, 16)

        @block.tensor
        def _(pe):
            here = Place(NAMES)
            pe.sem_inc(unit_done, 4)
            for s in (*acc_free, *tp_free, *sc_free):
                pe.sem_inc(s, 1)
            pe.wait_ge(ready, 1)

            def unit(u, a_hi, a_lo, kts, w, pair, first, last):
                if first:
                    pe.wait_ge(acc_free[pair], here.next(f"acc{pair}"))
                pe.wait_ge(lo_ready, here.next("unit") + 8)
                for dk, kt in enumerate(kts):
                    for t in range(T):
                        o = acc[:, pair, t, 0:w]
                        a1, a2 = a_hi[:, kt, t * P:(t + 1) * P], a_lo[:, kt, t * P:(t + 1) * P]
                        w1, w2 = hi[:, u % 4, dk, 0:w], lo[:, u % 4, dk, 0:w]
                        pe.matmul(o, a1, w1, start=first and dk == 0, stop=False)
                        pe.matmul(o, a1, w2, start=False, stop=False)
                        mm = pe.matmul(o, a2, w1, start=False, stop=last and dk == 1)
                mm.then_inc(unit_done, 1)

            def fill(name, tiles):
                b = here.fill(name)
                pe.wait_ge(tp_free[b], here.now(f"tp{b}"))
                if tiles[0].shape[0] < P:
                    pe.sem_inc(waited, 1)
                for i, tile in enumerate(tiles):
                    k, m = tile.shape
                    mm = pe.transpose(tp[0:m, b, i, 0:k], tile, ident[0:k, 0:k])
                mm.then_inc(tp_full, 1)

            def emptied(*names):
                for name in names:
                    b, value = here.emptied(name)
                    pe.wait_ge(tp_free[b], value)

            def norm_fills():
                for t in range(T):
                    pe.wait_ge(normed, here.next("normed"))
                    for i in range(KT // 4):
                        fill(("norm", t, i), [wide[:, k * P:(k + 1) * P] for k in range(4 * i, 4 * i + 4)])

            def scores(bank, pairs):
                pe.wait_ge(sc_free[bank], here.next(f"sc{bank}"))
                for t, (a, b) in enumerate(pairs):
                    mm = pe.matmul(sc[:, bank, t, :], a, b, start=(t == 0), stop=(t == T - 1),
                                   skip_group_check=True)
                mm.then_inc(sc_full, 1)

            def head_output(j):
                emptied(("p", j, 0))
                b = here.fill(("o", j, 0))
                pe.wait_ge(tp_free[b], here.now(f"tp{b}"))
                o = tp[:, b, 0:2, :].rearrange("p a d -> p (a d)")
                for kt in range(T):
                    if j < MEM_HEADS:
                        v = mv_tok[:, kt, j]
                    else:
                        v = kv_tok[:, kt, KV_HEADS + (j - MEM_HEADS) // (HEADS // KV_HEADS)]
                    mm = pe.matmul(o, v, pT[:, j % 2, kt, :], start=(kt == 0), stop=(kt == T - 1))
                mm.then_inc(tp_full, 1)

            def side(n):
                for _, what, i, j in [f for f in FILLS if f[0] == n]:
                    name = (what, i, j)
                    if what == "taps":
                        pe.wait_ge(front_in, here.next("front_in", 16 * FRONT_DMAS))
                        pe.sem_inc(waited, 1)
                        fill(name, [tap_rows[:, c * P:(c + 1) * P] for c in range(CONV // P)])
                    elif what == "mem":
                        if j == 0:
                            pe.wait_ge(normed, here.next("normed"))
                        fill(name, [wide[:, k * P:(k + 1) * P] for k in range(4 * j, 4 * j + 4)])
                    elif what == "ik":
                        pe.wait_ge(ik_turned, here.next("ik_turned"))
                        fill(name, [ik_twice[:, t].rearrange("p a d -> p (a d)") for t in range(T)])
                    elif what == "iq":
                        if j == 0:
                            pe.wait_ge(iq_turned, here.next("iq_turned"))
                        two = iq_tok[:, j].rearrange("p (g a) d -> p g (a d)", a=2)
                        fill(name, [two[:, g] for g in range(4 * i, 4 * i + 4)])
                    elif what == "conv_in":
                        if i == 0:
                            pe.wait_ge(glu_done, here.next("glu_done"))
                        fill(name, [glu_a[:, i, c * P:(c + 1) * P] for c in range(CONV // P)])
                    elif what in ("mk", "mq"):
                        if i == 0:
                            pe.wait_ge(rows_ready, here.next("rows_ready"))
                        fill(name, [(mk_tok if what == "mk" else mq_tok)[:, i, h] for h in range(MEM_HEADS)])
                    elif what == "k":
                        if i == 0:
                            pe.wait_ge(rows_ready, here.next("rows_ready"))
                        fill(name, [kv_tok[:, t, i] for t in range(T)])
                    elif what == "q":
                        if j == 0:
                            pe.wait_ge(rows_ready, here.next("rows_ready"))
                        fill(name, [q_tok[:, j, h] for h in range(4 * i, 4 * i + 4)])
                    elif what == "conv_out":
                        if i == 0:
                            pe.wait_ge(conv_done, here.next("conv_done"))
                        fill(name, [conv_acc[:, c, i * P:(i + 1) * P] for c in range(CONV // P)])
                    elif what == "conv_row":
                        if i == 0:
                            pe.wait_ge(swish_done, here.next("swish_done"))
                        fill(name, [y_tok[:, i, c * P:(c + 1) * P] for c in range(CONV // P)])
                    elif what == "p":
                        pe.wait_ge(probs, here.next("probs"))
                        fill(name, [s_buf[:, i % 3, t, k * P:(k + 1) * P] for k in range(T) for t in range(T)])
                    elif what == "o":
                        head_output(i)
                if INDEX_AT <= n < INDEX_AT + IDX_HEADS:
                    j, a = divmod(n - INDEX_AT, 2)
                    if n == INDEX_AT:
                        emptied(("ik", 0, 0), ("iq", 1, 1))
                    half = slice(a * IDX_DIM, (a + 1) * IDX_DIM)
                    scores(a, [(iqT[half, j, t * P:(t + 1) * P], ikT[half, :]) for t in range(T)])
                if n in HEAD_AT:
                    j = HEAD_AT.index(n)
                    h = j - MEM_HEADS
                    if j == 0:
                        emptied(("mk", 1, 0), ("mq", 1, 0))
                    if h == 0:
                        emptied(("k", 1, 0), ("q", 0, 1))
                    if h == 4:
                        emptied(("q", 1, 1))
                    for_head = (mqT[:, j], mkT[:, j]) if h < 0 else (qT[:, h], kT[:, h // 4])
                    scores(j % 2, [(for_head[0][:, t * P:(t + 1) * P], for_head[1]) for t in range(T)])

            def merge(first):
                for m in range(4 * UNITS):
                    if m < 24:
                        g, u = divmod(m, UNITS)
                        unit(u, hT_hi, hT_lo, (2 * u, 2 * u + 1), COL, (1, 0, 1)[g], u == 0, u == UNITS - 1)
                    elif m < 26:
                        if first and m == 24:
                            emptied(("conv_row", 1, 0))
                        u = m - 24
                        unit(m % 8, cT_hi, cT_lo, (2 * u, 2 * u + 1), COL, 0, u == 0, u == 1)
                    elif m < 28:
                        if first and m == 26:
                            emptied(("o", MEM_HEADS - 1, 0))
                        u = m - 26
                        unit(m % 8, moT_hi, moT_lo, (2 * u, 2 * u + 1), COL, 1, u == 0, u == 1)
                    else:
                        if first and m == 28:
                            emptied(("o", MEM_HEADS + HEADS - 1, 0))
                        u = m - 28
                        unit(m % 8, oT_hi, oT_lo, (2 * u, 2 * u + 1), COL, 0, u == 0, u == 3)
                    if first:
                        side(FRONT * UNITS + m)
                    else:
                        merged_fill(m - 7)

            def merged_fill(t):
                if t == 0:
                    pe.wait_ge(merged_ready, here.next("merged_ready"))
                if t in range(T):
                    fill(("merged", t), [merged[:, t, k * P:(k + 1) * P] for k in range(4)])

            def mlp(first):
                for m in range(8 * UNITS):
                    g, u = divmod(m, UNITS)
                    pair = (1, 0)[g % 2]
                    if g < CB:
                        unit(u, hT_hi, hT_lo, (2 * u, 2 * u + 1), COL, pair, u == 0, u == UNITS - 1)
                    else:
                        if m == 32:
                            emptied(("hidden", 2, 1))
                        if m == 38:
                            emptied(("hidden", 3, 1))
                        unit(u, bT_hi, bT_lo, (2 * u, 2 * u + 1), COL, pair, u == 0, u == UNITS - 1)
                    b, t = divmod(m - 11, UNITS)
                    if b in range(CB) and t in range(T):
                        if t == 0:
                            pe.wait_ge(hid_ready, here.next("hid_ready"))
                        fill(("hidden", b, t), [hidden[:, b % 2, t, k * P:(k + 1) * P] for k in range(4)])

            with pe.Fori(0, LAYERS) as l, here.loop("layer", l, 0, LAYERS):
                norm_fills()
                emptied(("norm", 1, 2), ("norm", 1, 3))
                for n in range(FRONT * UNITS):
                    g, u = divmod(n, UNITS)
                    if n == G_MK * UNITS:
                        emptied(("mem", 1, 3))
                    a = (bT_hi, bT_lo) if g in (G_MK, G_MV) else (hT_hi, hT_lo)
                    unit(u, *a, (2 * u, 2 * u + 1), width_of(g), g % 2, u == 0, u == UNITS - 1)
                    side(n)
                merge(True)
                with pe.Fori(1, CB) as c, here.loop("merge", c, 1, CB - 1):
                    merge(False)
                for m in range(CB * UNITS):
                    g, u = divmod(m, UNITS)
                    if m == 6:
                        emptied(("merged", 1))
                    unit(u, bT_hi, bT_lo, (2 * u, 2 * u + 1), COL, (1, 0)[g % 2], u == 0, u == UNITS - 1)
                    merged_fill(m - 3)
                norm_fills()
                emptied(("norm", 1, 2), ("norm", 1, 3))
                mlp(True)
                with pe.Fori(1, FFN // D) as qu, here.loop("ffn", qu, 1, FFN // D - 1):
                    mlp(False)

        @block.scalar
        def _(act):
            here = Place(NAMES)

            def alone():
                act.sem_inc(waited, 1)

            def split(u, w):
                c = u // 2
                if u % 2 == 0:
                    if u == 0:
                        here.next("group")
                    act.wait_ge(landed[c], here.now("group") * 16)
                act.wait_ge(unit_done, here.next("unit"))
                act.activation(hi[:, u % 4, :, 0:w], raw[:, c, 2 * (u % 2):2 * (u % 2) + 2, 0:w],
                               ACT.Copy).then_inc(hi_ready, 1)

            def take(name, out_ap, n=4, w=P, parts=P):
                act.wait_ge(tp_full, here.next("fill"))
                b = here.fill(name)
                act.activation(out_ap, tp[0:parts, b, 0:n, 0:w], ACT.Copy).then_inc(tp_free[b], 1)

            def take_high(name, out_ap, n=4):
                act.wait_ge(tp_full, here.next("fill"))
                b = here.fill(name)
                act.activation(out_ap, tp[:, b, 0:n, :], ACT.Copy).then_inc(tp_hi, 1)

            def square_sum(source, sums):
                if here.n["squared"] or here.base["squared"].__class__ is not int:
                    act.wait_ge(squared, here.now("squared"))
                here.next("squared")
                act.activation(sc[:, 1].rearrange("p t s -> p (t s)"), source, ACT.Square,
                               accum_out=sums).then_inc(squared, 1)

            def norm_fills():
                for t in range(T):
                    for i in range(KT // 4):
                        take_high(("norm", t, i), hT_hi[:, 4 * i:4 * i + 4, t * P:(t + 1) * P])

            def block_done(e):
                act.wait_ge(unit_done, origin[0] + e + 5)

            def side(n):
                for _, what, i, j in [f for f in FILLS if f[0] + EMPTY_AFTER == n]:
                    name = (what, i, j)
                    cols = slice(i * P, (i + 1) * P)
                    if what == "taps":
                        take(name, tapT[:, :, :], w=TAPS + 1)
                    elif what == "mem":
                        take_high(name, bT_hi[:, 4 * j:4 * j + 4, cols])
                    elif what == "ik":
                        take(name, ikT[:, :].rearrange("p (t s) -> p t s", t=T), n=2)
                    elif what == "iq":
                        take(name, iqT[:, 4 * i:4 * i + 4, j * P:(j + 1) * P])
                    elif what == "conv_in":
                        if i == 0:
                            act.wait_ge(pad_ready, here.next("pad_ready"))
                        take(name, uT[:, :, TAPS - 1 + i * P:TAPS - 1 + (i + 1) * P])
                    elif what == "mk":
                        take(name, mkT[:, :, cols])
                    elif what == "mq":
                        take(name, mqT[:, :, cols])
                    elif what == "k":
                        take(name, kT[:, i].rearrange("p (t s) -> p t s", t=T), n=2)
                    elif what == "q":
                        take(name, qT[:, 4 * i:4 * i + 4, j * P:(j + 1) * P])
                    elif what == "conv_out":
                        take(name, y_tok[:, i].rearrange("p (c s) -> p c s", s=P))
                    elif what == "conv_row":
                        take_high(name, cT_hi[:, :, cols])
                    elif what == "p":
                        take(name, pT[:, i % 2].rearrange("p k (t s) -> p (k t) s", t=T))
                    elif what == "o":
                        o = moT_hi[:, i] if i < MEM_HEADS else oT_hi[:, i - MEM_HEADS]
                        take_high(name, o.rearrange("p (t s) -> p t s", t=T), n=2)
                if n == IKW_TAKEN:
                    block_done(G_IKW * UNITS + 7)
                    act.activation(ikw_tok[:, :, :], acc[:, 0, :, 0:IKW], ACT.Copy).then_inc(acc_free[0], 1)
                for i, g in enumerate((G_IQ0, G_IQ1)):
                    if n == IQ_TAKEN[i]:
                        if i == 0:
                            act.wait_ge(parked, here.next("parked", 32))
                        block_done(g * UNITS + 7)
                        act.activation(iq_tok[:, :, 8 * i:8 * i + 8, :].rearrange("p t h d -> p t (h d)"),
                                       acc[:, g % 2], ACT.Copy).then_inc(acc_free[g % 2], 1)
                if n in MEM_SQUARES:
                    act.wait_ge(mem_in, here.next("mem_in", 16))
                    t = MEM_SQUARES.index(n)
                    for b in range(CB):
                        square_sum(wide[:, b * COL:(b + 1) * COL], mem_sum[:, t, b:b + 1])
                s = n - INDEX_AT - EMPTY_AFTER
                if s in range(IDX_HEADS):
                    act.wait_ge(sc_full, here.next("score"))
                    if s >= 2:
                        act.wait_ge(relu_used, here.next("relu_used"))
                    act.activation(relu[:, s % 2], sc[:, s % 2], ACT.Relu).then_inc(sc_free[s % 2], 1)
                    if s == IDX_HEADS - 1:
                        here.next("relu_used", 2)
                if n == GLU_EXP:
                    act.wait_ge(glu_here, here.next("glu_here"))
                    act.activation(glu_g[:, :, :], glu_g[:, :, :], ACT.Exp, scale=-1.0).then_inc(glu_exp, 1)
                if n in ROWS_TAKEN:
                    k = ROWS_TAKEN.index(n)
                    g, dest, heads = ROWS[k]
                    block_done(g * UNITS + 7)
                    src = acc[:, g % 2].rearrange("p t (h d) -> p t h d", d=HEAD)
                    if k > 0:
                        act.wait_ge(head_mean, here.next("head_mean"))
                    act.activation(squares[:, :, 0:heads * HEAD], acc[:, g % 2, :, 0:heads * HEAD],
                                   ACT.Square)
                    act.activation(dest, src, ACT.Copy).then_inc(rows_here, 1)
                    act.wait_ge(rows_here, here.next("rows_here"))
                    act.sem_inc(acc_free[g % 2], 1)
                    if k == len(ROWS) - 1:
                        here.next("head_mean")
                if n == MV_TAKEN:
                    block_done(G_MV * UNITS + 7)
                    act.activation(mv_tok[:, :, :, :].rearrange("p t h d -> p t (h d)"), acc[:, G_MV % 2],
                                   ACT.Copy).then_inc(acc_free[G_MV % 2], 1)
                if n - 5 in HEAD_AT:
                    r = HEAD_AT.index(n - 5) % 3
                    act.wait_ge(logits, here.next("logits"))
                    for t in range(T):
                        e = act.activation(s_buf[:, r, t], s_buf[:, r, t], ACT.Exp, bias=neg_max[:, r, t:t + 1],
                                           accum_out=p_sum[:, r, t:t + 1])
                    e.then_inc(exps, 1)
                if n == Y_EXP:
                    act.wait_ge(ln_scaled, here.next("ln_scaled"))
                    act.activation(y_sig[:, :, :], y_tok[:, :, :], ACT.Exp, scale=-1.0).then_inc(y_exp, 1)

            def merged_take(t, cols):
                if t in range(T):
                    act.wait_ge(tp_full, here.next("fill"))
                    alone()
                    b = here.fill(("merged", t))
                    act.activation(bT_hi[:, cols, t * P:(t + 1) * P], tp[:, b], ACT.Copy).then_inc(tp_hi, 1)

            def merge(first, c):
                for m in range(4 * UNITS):
                    split(m % UNITS, COL)
                    if first:
                        side(FRONT * UNITS + m)
                    else:
                        merged_take(m - 11, bass.ds((c - 1) * 4, 4))
                    if m in GATE_EXP:
                        i = GATE_EXP.index(m)
                        act.wait_ge(gate_in, here.next("gate_in"))
                        act.activation(gates[:, i], gates[:, i], ACT.Exp, scale=-1.0).then_inc(gate_exp, 1)

            def x_squares(b):
                act.wait_ge(x_new, here.next("x_new"))
                for t in range(T):
                    square_sum(x_tok[:, t, b * COL:(b + 1) * COL], sq_sum[:, t, b:b + 1])

            def mlp(first):
                for m in range(8 * UNITS):
                    if not (first and m < 4):
                        split(m % UNITS, COL)
                    if m == 5 and not first:
                        x_squares(CB - 1)
                    b, r = divmod(m - 12, UNITS)
                    if r == 0 and b in range(CB):
                        block_done(b * UNITS + 7)
                        act.activation(hidden[:, b % 2], acc[:, (1, 0)[b % 2]], ACT.Relu).then_inc(hid_relu, 1)
                        act.wait_ge(hid_relu, here.next("hid_relu"))
                        act.sem_inc(acc_free[(1, 0)[b % 2]], 1)
                    b, t = divmod(m - 15, UNITS)
                    if b in range(CB) and t in range(T):
                        take_high(("hidden", b, t), bT_hi[:, 4 * b:4 * b + 4, t * P:(t + 1) * P])
                    if m in (45, 53, 61):
                        x_squares((m - 45) // 8)

            origin = [0]
            act.wait_ge(ready, 4)
            act.activation(sin[:, :, :], angle[:, :, :], ACT.Sin).then_inc(act_step, 1)
            act.activation(cos[:, :, :], fold[:, :, :], ACT.Sin, scale=-1.0,
                           bias=half_pi[:, 0:1]).then_inc(act_step, 1)
            here.next("act_step", 2)
            act.wait_ge(x_in, 48)
            for b in range(CB):
                for t in range(T):
                    square_sum(x_tok[:, t, b * COL:(b + 1) * COL], sq_sum[:, t, b:b + 1])
            with act.Fori(0, LAYERS) as l, here.loop("layer", l, 0, LAYERS):
                origin[0] = here.now("unit")
                for u in range(4):
                    split(u, IKW)
                norm_fills()
                for n in range(FRONT * UNITS):
                    if n >= 4:
                        split(n % UNITS, width_of(n // UNITS))
                    side(n)
                merge(True, 0)
                with act.Fori(1, CB) as c, here.loop("merge", c, 1, CB - 1):
                    merge(False, c)
                for m in range(CB * UNITS):
                    split(m % UNITS, COL)
                    merged_take(m - 7, slice(KT - 4, KT))
                    if m in (13, 21, 29):
                        x_squares((m - 13) // 8)
                x_squares(CB - 1)
                here.next("score", MEM_HEADS + HEADS)
                origin[0] = here.now("unit")
                for u in range(4):
                    split(u, COL)
                norm_fills()
                mlp(True)
                with act.Fori(1, FFN // D) as qu, here.loop("ffn", qu, 1, FFN // D - 1):
                    origin[0] = here.now("unit")
                    mlp(False)
                x_squares(CB - 1)

        @block.vector
        def _(dve):
            here = Place(NAMES)
            origin = [0]

            def step(ins):
                ins.then_inc(dve_step, 1)
                here.next("dve_step")

            def settle(back=0):
                dve.wait_ge(dve_step, here.now("dve_step") - back)

            def link(ins):
                step(ins)
                settle()

            def alone():
                dve.sem_inc(waited, 1)

            def split(u, w):
                dve.wait_ge(hi_ready, here.next("unit"))
                dve.tensor_tensor(lo[:, u % 4, :, 0:w], raw[:, u // 2, 2 * (u % 2):2 * (u % 2) + 2, 0:w],
                                  hi[:, u % 4, :, 0:w].bitcast(F32), ALU.subtract).then_inc(lo_ready, 1)

            def take_low(name, dst, src, n=4):
                b = here.fill(name)
                dve.wait_ge(tp_hi, here.next("tp_hi"))
                dve.tensor_tensor(dst, tp[:, b, 0:n, :], src.bitcast(F32), ALU.subtract).then_inc(tp_free[b], 1)

            def means(t, sums, count):
                dve.wait_ge(squared, here.next("squared", count))
                link(dve.tensor_reduce(mean_sq[:, t:t + 1], sums[:, t], AX_X, ALU.add))
                dve.tensor_scalar(mean_sq[:, t:t + 1], mean_sq[:, t:t + 1], 1.0 / D, EPS, ALU.mult,
                                  ALU.add).then_inc(mean_ready, 1)

            def normalise(t, source, fresh_gain):
                if fresh_gain:
                    dve.wait_ge(gain_in, here.next("gain_in", 16))
                dve.wait_ge(rstd_ready, here.next("rstd_ready"))
                dve.scalar_tensor_tensor(wide[:, :], source, rstd[:, t:t + 1], gain[:, :], ALU.mult,
                                         ALU.mult).then_inc(normed, 1)

            def norm_start(w):
                means(0, sq_sum, T * CB)
                means(1, sq_sum, 0)
                normalise(0, x_tok[:, 0], True)
                for u in range(2):
                    split(u, w)
                for t in range(T):
                    if t == 1:
                        dve.wait_ge(tp_full, here.now("fill") + 4)
                        normalise(1, x_tok[:, 1], False)
                        for u in range(2, 4):
                            split(u, w)
                    for i in range(KT // 4):
                        cols = slice(t * P, (t + 1) * P)
                        take_low(("norm", t, i), hT_lo[:, 4 * i:4 * i + 4, cols], hT_hi[:, 4 * i:4 * i + 4, cols])
                here.next("fill", 8)

            def block_done(e):
                dve.wait_ge(unit_done, origin[0] + e + 5)

            def conv_taps(n):
                k = n - CONV_AT
                if k not in range(TAPS):
                    return
                if k == 0:
                    for name in (("taps", 0, 0), ("conv_in", 1, 0)):
                        b, value = here.emptied(name)
                        dve.wait_ge(tp_free[b], value)
                for c in range(CONV // P):
                    src = uT[:, c, k:k + SEQ]
                    if k == 0:
                        step(dve.tensor_scalar(conv_acc[:, c], src, tapT[:, c, 0:1], tapT[:, c, TAPS:TAPS + 1],
                                               ALU.mult, ALU.add))
                    else:
                        settle(CONV // P - 1)
                        step(dve.scalar_tensor_tensor(conv_acc[:, c], src, tapT[:, c, k:k + 1], conv_acc[:, c],
                                                      ALU.mult, ALU.add))
                if k == TAPS - 1:
                    settle()
                    dve.sem_inc(conv_done, 1)

            def select_round(r):
                if r == 0:
                    dve.wait_ge(causal_done, here.next("causal_done"))
                    alone()
                for t in range(T):
                    keys = (t + 1) * P
                    step(dve.max(top8[:, t], index[:, t, 0:keys]))
                for t in range(T):
                    keys = (t + 1) * P
                    settle(1 if t == 0 else 1)
                    alone()
                    step(dve.match_replace(index[:, t, 0:keys], top8[:, t], index[:, t, 0:keys], TAKEN))
                settle()
                alone()

            def head(j):
                r = j % 3
                dve.wait_ge(sc_full, here.next("score"))
                if j >= 3:
                    dve.wait_ge(tp_full, fill_count[("p", j - 3, 0)] + here.base["fill"])
                if j < MEM_HEADS:
                    ins = dve.tensor_scalar(s_buf[:, r], sc[:, j % 2], SCALE, None, ALU.mult)
                else:
                    if j == MEM_HEADS:
                        dve.wait_ge(causal_done, here.next("causal_done"))
                    ins = dve.scalar_tensor_tensor(s_buf[:, r], sc[:, j % 2], SCALE, mask[:, :, :], ALU.mult,
                                                   ALU.add)
                ins.then_inc(sc_free[j % 2], 1)
                here.next(f"sc{j % 2}")
                dve.wait_ge(sc_free[j % 2], here.now(f"sc{j % 2}") + 1)
                dve.tensor_reduce(neg_max[:, r], s_buf[:, r], AX_X, ALU.max, negate=True).then_inc(logits, 1)

            def side(n):
                for _, what, i, j in [f for f in FILLS if f[0] + EMPTY_AFTER == n]:
                    here.next("fill")
                    name = (what, i, j)
                    fill_count[name] = here.n["fill"]
                    cols = slice(i * P, (i + 1) * P)
                    if what == "mem":
                        take_low(name, bT_lo[:, 4 * j:4 * j + 4, cols], bT_hi[:, 4 * j:4 * j + 4, cols])
                    elif what == "conv_row":
                        take_low(name, cT_lo[:, :, cols], cT_hi[:, :, cols])
                    elif what == "o":
                        h, l_ = (moT_hi[:, i], moT_lo[:, i]) if i < MEM_HEADS else \
                            (oT_hi[:, i - MEM_HEADS], oT_lo[:, i - MEM_HEADS])
                        take_low(name, l_.rearrange("p (t s) -> p t s", t=T),
                                 h.rearrange("p (t s) -> p t s", t=T), n=2)
                    else:
                        here.fill(name)
                for t in range(T):
                    if n == MEM_MEAN[t]:
                        means(t, mem_sum, CB)
                    if n == MEM_NORM[t]:
                        normalise(t, wide[:, :], t == 0)
                if n - INDEX_AT - EMPTY_AFTER in range(IDX_HEADS):
                    s = n - INDEX_AT - EMPTY_AFTER
                    if s == 0:
                        dve.wait_ge(ik_turned, here.next("ik_turned"))
                    here.next(f"sc{s % 2}")
                    dve.wait_ge(sc_free[s % 2], here.now(f"sc{s % 2}") + 1)
                    for t in range(T):
                        w = iw[:, t, s:s + 1]
                        if s == 0:
                            ins = dve.tensor_scalar(index[:, t], relu[:, 0, t], w, None, ALU.mult)
                        else:
                            ins = dve.scalar_tensor_tensor(index[:, t], relu[:, s % 2, t], w, index[:, t],
                                                           ALU.mult, ALU.add)
                    ins.then_inc(relu_used, 1)
                    dve.wait_ge(relu_used, here.next("relu_used"))
                    here.next("score")
                if n == GLU_A_TAKEN:
                    dve.wait_ge(front_in, here.next("front_in", 16 * FRONT_DMAS))
                    block_done(G_GLUA * UNITS + 7)
                    dve.tensor_tensor(glu_a[:, :, :], acc[:, G_GLUA % 2], over(glu_b[:, 0], 1, T),
                                      ALU.add).then_inc(acc_free[G_GLUA % 2], 1)
                if n == GLU_G_TAKEN:
                    block_done(G_GLUG * UNITS + 7)
                    dve.tensor_tensor(glu_g[:, :, :], acc[:, G_GLUG % 2], over(glu_b[:, 1], 1, T),
                                      ALU.add).then_inc(glu_here, 1)
                    dve.wait_ge(glu_here, here.next("glu_here"))
                    dve.sem_inc(acc_free[G_GLUG % 2], 1)
                if n == GLU_EXP + 1:
                    dve.wait_ge(glu_exp, here.next("glu_exp"))
                    link(dve.tensor_scalar(glu_g[:, :, :], glu_g[:, :, :], 1.0, None, ALU.add))
                    link(dve.reciprocal(glu_g[:, :, :], glu_g[:, :, :]))
                if n == GLU_EXP + 2:
                    dve.tensor_tensor(glu_a[:, :, :], glu_a[:, :, :], glu_g[:, :, :],
                                      ALU.mult).then_inc(glu_done, 1)
                conv_taps(n)
                r, rest = divmod(n - TOPK_AT, 3)
                if rest == 0 and r in range(TOPK // 8):
                    select_round(r)
                if rest == 1 and r == TOPK // 8 - 1:
                    dve.tensor_scalar(mask[:, :, :], index[:, :, :], TAKEN, -BIG, ALU.not_equal,
                                      ALU.mult).then_inc(chosen, 1)
                if n - 1 in ROWS_TAKEN:
                    k = ROWS_TAKEN.index(n - 1)
                    _, dest, heads = ROWS[k]
                    dve.wait_ge(rows_here, here.next("rows_here"))
                    if k > 0:
                        dve.wait_ge(rows_ready, here.next("rows_ready"))
                    link(dve.tensor_reduce(head_sum[:, 0:T * heads].rearrange("p (t h) -> p t h", t=T),
                                           squares[:, :, 0:heads * HEAD].rearrange("p t (h d) -> p t h d", d=HEAD),
                                           AX_X, ALU.add))
                    dve.tensor_scalar(head_sum[:, 0:T * heads], head_sum[:, 0:T * heads], 1.0 / HEAD, EPS,
                                      ALU.mult, ALU.add).then_inc(head_mean, 1)
                    if k == len(ROWS) - 1:
                        here.next("rows_ready")
                if n - 4 in HEAD_AT:
                    head(HEAD_AT.index(n - 4))
                if n - 6 in HEAD_AT:
                    r = HEAD_AT.index(n - 6) % 3
                    dve.wait_ge(exps, here.next("exps"))
                    dve.reciprocal(p_inv[:, r], p_sum[:, r]).then_inc(inv_ready, 1)
                if n == LN_STATS:
                    b, value = here.emptied(("conv_out", 1, 0))
                    dve.wait_ge(tp_free[b], value)
                    for t in range(T):
                        step(dve.bn_stats(bn[:, t], y_tok[:, t]))
                    settle()
                    alone()
                    for t in range(T):
                        step(dve.bn_aggr(mean_var[:, t], bn[:, t]))
                    settle()
                    dve.tensor_scalar(ln_rstd[:, :], mean_var[:, :, 1], EPS, None, ALU.add).then_inc(ln_stat, 1)
                if n == LN_APPLY:
                    dve.wait_ge(ln_root, here.next("ln_root"))
                    for t in range(T):
                        ins = dve.tensor_scalar(y_tok[:, t], y_tok[:, t], mean_var[:, t, 0:1], ln_rstd[:, t:t + 1],
                                                ALU.subtract, ALU.mult)
                    ins.then_inc(ln_done, 1)
                if n == Y_EXP + 1:
                    dve.wait_ge(y_exp, here.next("y_exp"))
                    link(dve.tensor_scalar(y_sig[:, :, :], y_sig[:, :, :], 1.0, None, ALU.add))
                    link(dve.reciprocal(y_sig[:, :, :], y_sig[:, :, :]))
                if n == Y_EXP + 2:
                    dve.tensor_tensor(y_tok[:, :, :], y_tok[:, :, :], y_sig[:, :, :],
                                      ALU.mult).then_inc(swish_done, 1)

            def attention_merge(e):
                block_done(e)
                link(dve.tensor_tensor(gates[:, 0], gates[:, 0], acc[:, 0], ALU.mult))
                dve.sem_inc(acc_free[0], 1)
                dve.tensor_tensor(merged[:, :, :], merged[:, :, :], gates[:, 0], ALU.add).then_inc(merged_ready, 1)

            def merged_low(t, cols):
                if t in range(T):
                    c = slice(t * P, (t + 1) * P)
                    here.next("fill")
                    take_low(("merged", t), bT_lo[:, cols, c], bT_hi[:, cols, c])

            def merge(first, c):
                for m in range(4 * UNITS):
                    split(m % UNITS, COL)
                    if first:
                        side(FRONT * UNITS + m)
                    else:
                        merged_low(m - 11, bass.ds((c - 1) * 4, 4))
                        if m == 4:
                            attention_merge(-1)
                    start = FRONT * UNITS if first else 0
                    if m in GATE_TAKEN:
                        i = GATE_TAKEN.index(m)
                        if i == 0:
                            dve.wait_ge(bias_in, here.next("bias_in", 32))
                        block_done(start + 8 * i + 7)
                        dve.tensor_tensor(gates[:, i], acc[:, (1, 0, 1)[i]], over(gate_bias[:, i], 1, T),
                                          ALU.add).then_inc(gate_in, 1)
                        dve.wait_ge(gate_in, here.next("gate_in"))
                        dve.sem_inc(acc_free[(1, 0, 1)[i]], 1)
                    if m == 29:
                        block_done(start + 25)
                        dve.tensor_tensor(merged[:, :, :], acc[:, 0], over(conv_bias[:, :], 1, T),
                                          ALU.add).then_inc(bias_used, 1)
                        dve.wait_ge(bias_used, here.next("bias_used"))
                        dve.sem_inc(acc_free[0], 1)
                    if m == 31:
                        block_done(start + 27)
                        link(dve.tensor_tensor(gates[:, 1], gates[:, 1], acc[:, 1], ALU.mult))
                        dve.sem_inc(acc_free[1], 1)
                    if m - 3 in GATE_TAKEN:
                        dve.wait_ge(gate_one, here.next("gate_one"))
                        i = GATE_TAKEN.index(m - 3)
                        link(dve.reciprocal(gates[:, i], gates[:, i]))
                    if m == 31:
                        link(dve.tensor_tensor(merged[:, :, :], merged[:, :, :], gates[:, 2], ALU.mult))
                        link(dve.tensor_tensor(merged[:, :, :], merged[:, :, :], gates[:, 1], ALU.add))

            def add_block(b, pair, e):
                block_done(e)
                xb = x_tok[:, :, b * COL:(b + 1) * COL]
                dve.tensor_tensor(xb, acc[:, pair], xb, ALU.add).then_inc(x_new, 1)
                dve.wait_ge(x_new, here.next("x_new"))
                dve.sem_inc(acc_free[pair], 1)

            def mlp(first):
                for m in range(8 * UNITS):
                    if not (first and m < 4):
                        split(m % UNITS, COL)
                    if m == 4 and not first:
                        add_block(CB - 1, 0, -1)
                    b, r = divmod(m - 13, UNITS)
                    if r == 0 and b in range(CB):
                        dve.wait_ge(hid_relu, here.next("hid_relu"))
                        dve.tensor_tensor(hidden[:, b % 2], hidden[:, b % 2], hidden[:, b % 2],
                                          ALU.mult).then_inc(hid_ready, 1)
                    b, t = divmod(m - 15, UNITS)
                    if b in range(CB) and t in range(T):
                        here.next("fill")
                        kts, cols = slice(4 * b, 4 * b + 4), slice(t * P, (t + 1) * P)
                        take_low(("hidden", b, t), bT_lo[:, kts, cols], bT_hi[:, kts, cols])
                    if m in (44, 52, 60):
                        b = (m - 44) // 8
                        add_block(b, (1, 0)[b % 2], 8 * b + 39)

            fill_count = {}
            dve.sem_inc(lo_ready, 8)
            dve.wait_ge(x_in, 48)
            dve.wait_ge(ready, 3)
            link(dve.tensor_copy(pos_f[:, :], pos_i[:, :]))
            for t in range(T):
                step(dve.tensor_scalar(angle[:, t], freq[:, :], pos_f[:, t:t + 1], None, ALU.mult))
            settle()
            link(dve.tensor_scalar(turns[:, :, :], angle[:, :, :], 1.0 / TWO_PI, ROUND, ALU.mult, ALU.add))
            link(dve.tensor_scalar(turns[:, :, :], turns[:, :, :], ROUND, None, ALU.subtract))
            for part in (PI_1, PI_2, PI_3):
                link(dve.scalar_tensor_tensor(angle[:, :, :], turns[:, :, :], -part, angle[:, :, :],
                                              ALU.mult, ALU.add))
            link(dve.tensor_scalar(angle[:, :, :], angle[:, :, :], PI_MAX, -PI_MAX, ALU.min, ALU.max))
            dve.scalar_tensor_tensor(fold[:, :, :], angle[:, :, :], -1.0, angle[:, :, :], ALU.mult,
                                     ALU.max).then_inc(ready, 1)
            with dve.Fori(0, LAYERS) as l, here.loop("layer", l, 0, LAYERS):
                origin[0] = here.now("unit")
                norm_start(IKW)
                for n in range(FRONT * UNITS):
                    if n >= 4:
                        split(n % UNITS, width_of(n // UNITS))
                    side(n)
                merge(True, 0)
                alone()
                with dve.Fori(1, CB) as c, here.loop("merge", c, 1, CB - 1):
                    origin[0] = here.now("unit")
                    merge(False, c)
                origin[0] = here.now("unit")
                for m in range(CB * UNITS):
                    split(m % UNITS, COL)
                    merged_low(m - 7, slice(KT - 4, KT))
                    if m == 4:
                        attention_merge(-1)
                    if m in (12, 20, 28):
                        if m == 12:
                            dve.wait_ge(x_back, here.next("x_back", 16))
                        b = (m - 12) // 8
                        add_block(b, (1, 0)[b % 2], 8 * b + 7)
                add_block(CB - 1, 0, 31)
                origin[0] = here.now("unit")
                norm_start(COL)
                mlp(True)
                with dve.Fori(1, FFN // D) as qu, here.loop("ffn", qu, 1, FFN // D - 1):
                    origin[0] = here.now("unit")
                    mlp(False)
                    here.next("squared", 2 * CB)
                origin[0] = here.now("unit")
                add_block(CB - 1, 0, -1)

        @block.gpsimd
        def _(pool):
            here = Place(NAMES)

            def link(ins):
                ins.then_inc(pool_step, 1)
                pool.wait_ge(pool_step, here.next("pool_step"))
                alone()

            def alone():
                pool.sem_inc(waited, 1)

            def rotate(rows_, half, f0):
                heads = rows_.shape[2]
                a, b = rows_[:, :, :, 0:half], rows_[:, :, :, half:2 * half]
                cs, sn = (over(tab[:, :, f0:f0 + half], 2, heads) for tab in (cos, sin))
                bs, as_ = (rope_tmp[:, i, 0:T * heads * half].rearrange("p (t h d) -> p t h d", t=T, h=heads)
                           for i in range(2))
                link(pool.tensor_tensor(bs, b, sn, ALU.mult))
                link(pool.tensor_tensor(as_, a, sn, ALU.mult))
                link(pool.tensor_tensor(a, a, cs, ALU.mult))
                link(pool.tensor_tensor(b, b, cs, ALU.mult))
                link(pool.tensor_tensor(a, a, bs, ALU.subtract))
                return pool.tensor_tensor(b, b, as_, ALU.add)

            def root(t):
                pool.wait_ge(mean_ready, here.next("mean_ready"))
                pool.tensor_tensor(rstd[:, t:t + 1], mean_sq[:, t:t + 1], minus_half[:, 0:1],
                                   ALU.pow).then_inc(rstd_ready, 1)

            def side(n, l):
                for t in range(T):
                    if n == MEM_MEAN[t]:
                        root(t)
                if n == IKW_TAKEN:
                    pool.wait_ge(acc_free[0], here.now("acc0") + 2)
                    alone()
                    link(pool.tensor_scalar(iw[:, :, :], ikw_tok[:, :, IDX_DIM:IKW], IDX_SCALE, None, ALU.mult))
                    link(rotate(ikw_tok[:, :, 0:IDX_DIM].unsqueeze(2), HALF_I, HALF_A))
                    pool.tensor_copy(ik_twice[:, :, :, :], over(ikw_tok[:, :, 0:IDX_DIM], 2, 2)
                                     ).then_inc(ik_turned, 1)
                if n == MEM_FILL[0][-1] + 1:
                    pool.wait_ge(tp_full, here.now("fill") + fills_until(("mem", 0, KT // 4 - 1)))
                    alone()
                    pool.dma_start(wide[:, :], mem_tokens[1]).then_inc(mem_in, 16)
                if n in IQ_TAKEN:
                    i = IQ_TAKEN.index(n)
                    g = (G_IQ0, G_IQ1)[i]
                    pool.wait_ge(acc_free[g % 2], here.now(f"acc{g % 2}") + 2 + g // 2)
                    alone()
                    rotate(iq_tok[:, :, 8 * i:8 * i + 8], HALF_I, HALF_A).then_inc(iq_turned, 1)
                if n - 1 in ROWS_TAKEN:
                    k = ROWS_TAKEN.index(n - 1)
                    _, dest, heads = ROWS[k]
                    dest = dest[:, :, 0:heads]
                    if k == 0:
                        pool.wait_ge(front_in, here.next("front_in", 16 * FRONT_DMAS))
                    pool.wait_ge(head_mean, here.next("head_mean"))
                    link(pool.tensor_tensor(head_rstd[:, 0:T * heads], head_sum[:, 0:T * heads],
                                            minus_half[:, 0:T * heads], ALU.pow))
                    link(pool.tensor_tensor(dest, dest, over(head_rstd[:, 0:T * heads].rearrange(
                        "p (t h) -> p t h", t=T), 3, HEAD), ALU.mult))
                    g = over(over(head_gain[:, (3, 2, 1, 0, 0)[k]], 1, heads), 1, T)
                    ins = pool.tensor_tensor(dest, dest, g, ALU.mult)
                    if k >= 2:
                        link(ins)
                        ins = rotate(dest, HALF_A, 0)
                    ins.then_inc(rows_ready, 1)
                if n == INDEX_AT + EMPTY_AFTER + IDX_HEADS - 1:
                    pool.wait_ge(relu_used, here.next("relu_used", IDX_HEADS))
                    alone()
                    pool.affine_select(out=index[:, :, :], in_=index[:, :, :], pattern=[[P, T], [-1, SEQ]],
                                       compare_op=ALU.is_ge, fill=UNSEEN, base=0,
                                       channel_multiplier=1).then_inc(causal_done, 1)
                if n == TOPK_AT + 3 * (TOPK // 8 - 1) + 1:
                    pool.wait_ge(chosen, here.next("chosen"))
                    alone()
                    pool.affine_select(out=mask[:, :, :], in_=mask[:, :, :], pattern=[[P, T], [-1, SEQ]],
                                       compare_op=ALU.is_ge, fill=-BIG, base=0,
                                       channel_multiplier=1).then_inc(causal_done, 1)
                if n == MASK_FREE:
                    pool.wait_ge(relu_used, here.now("relu_used"))
                    alone()
                    pool.dma_start(ln_g[:, :], rows(conv_ln_g[l])).then_inc(ln_in, 16)
                    pool.dma_start(ln_b[:, :], rows(conv_ln_b[l])).then_inc(ln_in, 16)
                if n - 6 in HEAD_AT:
                    r = HEAD_AT.index(n - 6) % 3
                    pool.wait_ge(inv_ready, here.next("inv_ready"))
                    pool.tensor_tensor(s_buf[:, r], s_buf[:, r], over(p_inv[:, r], 2, SEQ),
                                       ALU.mult).then_inc(probs, 1)
                if n == LN_STATS:
                    pool.wait_ge(ln_stat, here.next("ln_stat"))
                    pool.tensor_tensor(ln_rstd[:, :], ln_rstd[:, :], minus_half[:, 0:T], ALU.pow
                                       ).then_inc(ln_root, 1)
                if n == LN_APPLY:
                    pool.wait_ge(ln_in, here.next("ln_in", 32))
                    pool.wait_ge(ln_done, here.next("ln_done"))
                    link(pool.tensor_tensor(y_tok[:, :, :], y_tok[:, :, :], over(ln_g[:, :], 1, T), ALU.mult))
                    pool.tensor_tensor(y_tok[:, :, :], y_tok[:, :, :], over(ln_b[:, :], 1, T),
                                       ALU.add).then_inc(ln_scaled, 1)

            def biases(l, c):
                alone()
                pool.dma_start(gate_bias[:, :, :], rows(v_gb[l, :, bass.ds(c, COL)])).then_inc(bias_in, 16)
                pool.dma_start(conv_bias[:, :], rows(conv_o_b[l, bass.ds(c, COL)])).then_inc(bias_in, 16)

            def gate_ones(m):
                if m - 1 in GATE_EXP:
                    i = GATE_EXP.index(m - 1)
                    pool.wait_ge(gate_exp, here.next("gate_exp"))
                    alone()
                    pool.tensor_scalar(gates[:, i], gates[:, i], 1.0, None, ALU.add).then_inc(gate_one, 1)

            for t in range(T):
                pool.dma_start(x_tok[:, t], tokens[t]).then_inc(x_in, 16)
            pool.dma_start(pos_i[:, :], positions.rearrange("b (t p) -> p (b t)", p=P),
                           allow_slow_non_contiguous=True).then_inc(x_in, 16)
            link0 = pool.memset(ident[:, :], 0.0)
            link0.then_inc(pool_step, 1)
            here.next("pool_step")
            pool.wait_ge(pool_step, 1)
            pool.affine_select(out=ident[:, :], in_=ident[:, :], compare_op=ALU.not_equal, fill=1.0, base=0,
                               pattern=[[-1, P]], channel_multiplier=1).then_inc(ready, 1)
            for i in range(HALF_A):
                pool.memset(freq[:, i:i + 1], FREQ_A[i])
            for i in range(HALF_I):
                pool.memset(freq[:, HALF_A + i:HALF_A + i + 1], FREQ_I[i])
            pool.memset(half_pi[:, :], TWO_PI / 4).then_inc(ready, 1)
            pool.memset(minus_half[:, :], -0.5).then_inc(ready, 1)
            pool.wait_ge(act_step, 2)
            pool.wait_ge(x_in, 48)

            with pool.Fori(0, LAYERS) as l, here.loop("layer", l, 0, LAYERS):
                pool.wait_ge(squared, here.now("squared") + T * CB)
                alone()
                for t in range(T):
                    pool.dma_start(x_park[t], x_tok[:, t]).then_inc(parked, 16)
                pool.dma_start(gain[:, :], rows(norm1_g[l])).then_inc(gain_in, 16)
                pool.dma_start(tap_rows[0:TAPS, :], conv_w[l]).then_inc(front_in, 16)
                pool.dma_start(tap_rows[TAPS:TAPS + 1, :], conv_b[l].unsqueeze(0)).then_inc(front_in, 16)
                pool.dma_start(glu_b[:, :, :], rows(conv_in_b.rearrange("l (i n) -> l i n", i=2)[l])).then_inc(front_in, 16)
                for i, g in enumerate((q_norm_g, k_norm_g, mq_norm_g, mk_norm_g)):
                    pool.dma_start(head_gain[:, i], rows(g[l])).then_inc(front_in, 16)
                for t in range(T):
                    root(t)
                pool.memset(uT[:, :, 0:TAPS - 1], 0.0).then_inc(pad_ready, 1)
                pool.wait_ge(normed, here.next("normed", 2))
                alone()
                pool.dma_start(gain[:, :], rows(mem_norm_g[l])).then_inc(gain_in, 16)
                pool.wait_ge(tp_full, here.now("fill") + 8)
                alone()
                pool.dma_start(wide[:, :], mem_tokens[0]).then_inc(mem_in, 16)
                for n in range(FRONT * UNITS):
                    side(n, l)
                for m in range(4 * UNITS):
                    side(FRONT * UNITS + m, l)
                    if m == BIAS_AT:
                        pool.wait_ge(rows_ready, here.next("rows_ready", len(ROWS)))
                        pool.wait_ge(ln_stat, here.now("ln_stat"))
                        biases(l, 0)
                    gate_ones(m)
                with pool.Fori(1, CB) as c, here.loop("merge", c, 1, CB - 1):
                    for m in range(4 * UNITS):
                        if m == 0:
                            pool.wait_ge(bias_used, here.next("bias_used"))
                            biases(l, c * COL)
                        gate_ones(m)
                here.next("bias_used")
                pool.wait_ge(parked, here.next("parked", 32))
                pool.wait_ge(swish_done, here.next("swish_done"))
                alone()
                pool.dma_start(x_tok[:, :, :], x_park.rearrange("t p d -> p t d")).then_inc(x_back, 16)
                pool.wait_ge(tp_full, here.next("fill", NORM_FILLS + len(FILLS) + T))
                alone()
                pool.dma_start(gain[:, :], rows(norm2_g[l])).then_inc(gain_in, 16)
                for t in range(T):
                    root(t)
                here.next("normed", 4)
                here.next("x_new", 4 * 5)
                here.next("fill", 8 + 32)


INPUTS = ["x", "mem", "positions", "norm1_g", "w_in", "q_norm_g", "k_norm_g", "mem_norm_g", "w_mem_kv", "mq_norm_g",
          "mk_norm_g", "conv_in_b", "conv_w", "conv_b", "conv_ln_g", "conv_ln_b", "gate_b", "w_attn_o", "w_mem_o",
          "w_conv_o", "conv_o_b", "w_out", "norm2_g", "w_up", "w_down"]


def kernel(**inputs):
    import numpy as _np
    import concourse.bacc as _bacc
    from concourse import mybir as _mybir
    from concourse.bass_utils import run_bass_kernel_spmd as _run

    nc = _bacc.Bacc("TRN2", target_bir_lowering=False, num_devices=1)
    arrays, args = {}, []
    for name in INPUTS:
        a = _np.ascontiguousarray(inputs[name])
        arrays[f"in_{name}"] = a
        args.append(nc.dram_tensor(f"in_{name}", a.shape, _mybir.dt.from_np(a.dtype), kind="ExternalInput").ap())
    out = nc.dram_tensor("out", (1, SEQ, D), _mybir.dt.from_np(_np.dtype("float32")), kind="ExternalOutput").ap()
    build(nc, *args, out)
    r = _run(nc, [arrays], core_ids=[0])
    return r.results[0]["out"]
```

```python
from contextlib import ExitStack, contextmanager

import numpy as np

import concourse.bass as bass
from concourse import mybir

F32 = mybir.dt.float32
F32R = mybir.dt.float32r
I32 = mybir.dt.int32
ALU = mybir.AluOpType
ACT = mybir.ActivationFunctionType
AX_X = mybir.AxisListType.X

P = 128
LAYERS = 2
SEQ = 256
T = SEQ // P
D = 2048
KT = D // P
HEAD = 128
HEADS, KV_HEADS, MEM_HEADS = 8, 2, 4
IDX_HEADS, IDX_DIM = 16, 64
TOPK = 64
CONV = 512
TAPS = 31
FFN = 4 * D
EPS = 1e-6
COL = 512
CB = D // COL
SCALE = float(HEAD) ** -0.5
IDX_SCALE = float(IDX_DIM) ** -0.5 * float(IDX_HEADS) ** -0.5

Q0 = 0
K0 = Q0 + HEADS * HEAD
V0 = K0 + KV_HEADS * HEAD
IQ0 = V0 + KV_HEADS * HEAD
IK0 = IQ0 + IDX_HEADS * IDX_DIM
IW0 = IK0 + IDX_DIM
GLU0 = IW0 + IDX_HEADS
MQ0 = GLU0 + 2 * CONV
GATE0 = MQ0 + MEM_HEADS * HEAD
IKW = IDX_DIM + IDX_HEADS

FRONT = 11
UNITS = 8
CHUNKS = 4
(G_IQ0, G_IKW, G_IQ1, G_GLUA, G_GLUG, G_MK, G_MV, G_MQ, G_KV, G_Q0, G_Q1) = range(FRONT)
PAIR = {g: i % 2 for i, g in enumerate((G_IQ1, G_GLUA, G_GLUG, G_MK, G_MV, G_MQ, G_KV, G_Q0, G_Q1))} | {G_IQ0: 1}
GROUPS = FRONT + 4 * CB + CB + 2 * FFN // COL

HALF_A, HALF_I = HEAD // 4 // 2, IDX_DIM // 4 // 2
THETA = 500000.0
TWO_PI = 6.283185307179586
PI_1 = 6.28125
PI_2 = 0.0019340515136718750
PI_3 = TWO_PI - PI_1 - PI_2
ROUND = 1.5 * 2.0 ** 23
PI_MAX = 3.1415925

UNSEEN = -(2.0 ** 127)
TAKEN = -1.5 * 2.0 ** 127
BIG = 1e30

NORM_FILL = [2, 3]
MEM_FILL = [[27, 28, 29, 30], [38, 39, 40, 41]]
TAPS_FILL = 33
MEM_LOAD = 16
IKW_FILL = [20, 21]
IK_FILL = 28
IQ_FILL = [[16, 17], [31, 32]]
INDEX_AT = 36
CONV_IN_FILL = [45, 46]
MK_FILL = [57, 58]
MQ_FILL = [73, 74]
K_FILL = [81, 82]
Q_FILL = [[90, 91], [97, 99]]
CONV_OUT_FILL = [93, 95]
CONV_ROW_FILL = [108, 109]
HEAD_AT = [79 + 2 * j for j in range(4)] + [92 + 2 * j for j in range(8)]
DVE_TILES = 3
CONV_AT = 56
DVE_CONV = [(51, 1), (52, 1), (53, 1), (54, 1), (55, 1)] + [(n, 2 + n % 2) for n in range(56, 92)]
TOPK_AT = 58


def front_fills():
    f = [(TAPS_FILL, "taps", 0, 0), (IK_FILL, "ik", 0, 0)]
    f += [(n, "ikw", t, 0) for t, n in enumerate(IKW_FILL)]
    f += [(n, "norm", CB - 1, t) for t, n in enumerate(NORM_FILL)]
    f += [(n, "k", h, 0) for h, n in enumerate(K_FILL)]
    f += [(MEM_FILL[t][i], "mem", t, i) for t in range(T) for i in range(KT // 4)]
    f += [(IQ_FILL[h][t], "iq", h, t) for h in range(2) for t in range(T)]
    f += [(n, "conv_in", t, 0) for t, n in enumerate(CONV_IN_FILL)]
    f += [(n, "mk", t, 0) for t, n in enumerate(MK_FILL)]
    f += [(n, "mq", t, 0) for t, n in enumerate(MQ_FILL)]
    f += [(Q_FILL[h][t], "q", h, t) for h in range(2) for t in range(T)]
    f += [(n, "conv_out", t, 0) for t, n in enumerate(CONV_OUT_FILL)]
    f += [(n, "conv_row", t, 0) for t, n in enumerate(CONV_ROW_FILL)]
    f += [(b + 6, "p", j, 0) for j, b in enumerate(HEAD_AT)]
    f += [(b + 9, "o", j, 0) for j, b in enumerate(HEAD_AT)]
    return sorted(f)


FILLS = front_fills()
EMPTY_AFTER = 4


def fills_until(name):
    return [f[1:] for f in FILLS].index(name) + 1


IKW_TAKEN, IQ_TAKEN = 19, [12, 27]
X_SQUARES, X_MEAN = 5, 6
MEM_SQUARES, MEM_SCALED, MEM_MEAN = [24, 35], [25, 36], 36
GLU_A_TAKEN, GLU_G_TAKEN, GLU_TANH = 36, 43, 44
ROWS_TAKEN = [52, 68, 76, 83, 91]
MV_TAKEN = 60
MASK_FREE = 60
LN_STATS, LN_APPLY, Y_TANH = 99, 100, 103
GATE_TAKEN, GATE_TANH = [12, 20, 27], [13, 21, 28]
X_BLOCK_DONE = [12 + 8 * b for b in range(CB - 1)]
BIAS_AT = 8
FRONT_DMAS = 7
FREQ_A = [float(np.float32(THETA) ** (np.float32(-2.0 * i) / np.float32(2 * HALF_A))) for i in range(HALF_A)]
FREQ_I = [float(np.float32(THETA) ** (np.float32(-2.0 * i) / np.float32(2 * HALF_I))) for i in range(HALF_I)]

PER = {
    "layer": {"group": GROUPS, "unit": GROUPS * UNITS, "acc0": 35, "acc1": 35, "fill": 112, "tp0": 56, "tp1": 56,
              "tp_hi": 78, "score": 28, "sc0": 15, "sc1": 14, "squared": 24, "x_new": 20,
              "dve_step": 153, "pool_step": 106, "gain_in": 48, "mem_in": 32, "front_in": 16 * FRONT_DMAS,
              "ln_in": 32, "bias_in": 32 * CB, "parked": 32, "x_back": 16, "mean_ready": 3, "rstd_ready": 3,
              "scaled": 10, "ik_here": 2, "ikwT_here": 1, "ik_turned": 1, "iq_turned": 2,
              "relu_used": IDX_HEADS, "causal_done": 2, "chosen": 1,
              "glu_here": 1, "glu_tanh": 1, "glu_done": 1, "pad_ready": 1, "conv_done": 1,
              "conv_start": 1, "conv_rest": 1, "ln_stat": 1,
              "ln_root": 1, "ln_done": 1, "ln_scaled": 1, "y_tanh_ready": 1, "swish_done": 1, "rows_here": 5,
              "head_mean": 5, "rows_ready": 5, "logits": 12, "exps": 12, "inv_ready": 12, "probs": 12,
              "gate_in": 12, "gate_tanh": 12, "bias_used": CB, "merged_ready": CB,
              "hid_relu": 16, "hid_ready": 16},
    "merge": {"group": 4, "unit": 32, "acc0": 3, "acc1": 3, "fill": 2, "tp0": 1, "tp1": 1, "tp_hi": 2,
              "dve_step": 4, "bias_in": 32, "gate_in": 3, "gate_tanh": 3, "bias_used": 1,
              "merged_ready": 1},
    "ffn": {"group": 8, "unit": 64, "acc0": 4, "acc1": 4, "fill": 8, "tp0": 4, "tp1": 4, "tp_hi": 8,
            "x_new": 4, "hid_relu": 4, "hid_ready": 4},
}


assert sum(count for _, count in DVE_CONV) >= TAPS * DVE_TILES


class Place:

    def __init__(self, names):
        self.base = dict.fromkeys(names, 0)
        self.n = dict.fromkeys(names, 0)
        self.bank = 0
        self.mark = {}
        self.counted = set()

    def now(self, name):
        return self.base[name] + self.n[name]

    def next(self, name, by=1):
        self.n[name] += by
        self.counted.add(name)
        return self.now(name)

    def fill(self, name):
        b = self.bank
        self.bank = 1 - b
        self.next(f"tp{b}")
        self.mark[name] = (b, self.n[f"tp{b}"])
        return b

    def emptied(self, name):
        b, k = self.mark[name]
        return b, self.base[f"tp{b}"] + k + 1

    @contextmanager
    def loop(self, kind, i, first, trips):
        base, n, bank = dict(self.base), dict(self.n), self.bank
        for name in self.base:
            per = PER[kind].get(name, 0)
            self.base[name] = base[name] + n[name] + (i - first) * per
            self.n[name] = 0
        yield
        assert self.bank == bank, kind
        for name in self.base:
            per = PER[kind].get(name, 0)
            assert name not in self.counted or self.n[name] == per, (kind, name, self.n[name])
            self.base[name] = base[name]
            self.n[name] = n[name] + trips * per


def build(nc, x, mem, positions, norm1_g, w_in, q_norm_g, k_norm_g, mem_norm_g, w_mem_kv, mq_norm_g,
          mk_norm_g, conv_in_b, conv_w, conv_b, conv_ln_g, conv_ln_b, gate_b, w_attn_o, w_mem_o,
          w_conv_o, conv_o_b, w_out, norm2_g, w_up, w_down, out):
    ctx = ExitStack()
    with ctx:
        kb = 1024
        base = (nc.sbuf_base + 31) // 32 * 32
        ctx.enter_context(nc.sbuf_tensor("arena", [P, nc.sbuf_usable_end - base - 64], mybir.dt.uint8))

        def at(name, shape, offset, dt=F32):
            n = 4
            for s in shape[1:]:
                n *= s
            assert base + offset + n <= nc.sbuf_usable_end, name
            return nc.alloc_sbuf_tensor_at(name, shape, dt, offset=base + int(offset))

        raw = at("raw", [P, CHUNKS, 4, COL], 0)
        hi = at("hi", [P, 4, 2, COL], 32 * kb, F32R)
        lo = at("lo", [P, 4, 2, COL], 48 * kb, F32R)
        hT_hi = at("hT_hi", [P, KT, SEQ], 64 * kb, F32R)
        hT_lo = at("hT_lo", [P, KT, SEQ], 80 * kb, F32R)
        bT_hi = at("bT_hi", [P, KT, SEQ], 96 * kb, F32R)
        bT_lo = at("bT_lo", [P, KT, SEQ], 112 * kb, F32R)
        B = 96 * kb
        mqT = at("mqT", [P, MEM_HEADS, SEQ], B)
        attn_pT = at("attn_pT", [P, 2, T, SEQ], B)
        q_tok = at("q_tok", [P, T, HEADS, HEAD], B + 4 * kb)
        qT = at("qT", [P, HEADS, SEQ], B + 12 * kb)
        kv_tok = at("kv_tok", [P, T, 2 * KV_HEADS, HEAD], B + 20 * kb)
        kT = at("kT", [P, KV_HEADS, SEQ], B + 24 * kb)
        s_buf = at("s_buf", [P, 3, T, SEQ], B + 26 * kb)
        X = 128 * kb
        x_tok = at("x_tok", [P, T, D], X)
        iq_tok = at("iq_tok", [P, T, IDX_HEADS, IDX_DIM], X)
        iqT = at("iqT", [P, IDX_HEADS // 2, SEQ], X + 8 * kb)
        mask = at("mask", [P, T, SEQ], X)
        ln_g = at("ln_g", [P, CONV], X + 2 * kb)
        ln_b = at("ln_b", [P, CONV], X + 4 * kb)
        y_tok = at("y_tok", [P, T, CONV], X + 6 * kb)
        tap_part = at("tap_part", [P, SEQ], X + 10 * kb)
        y_tanh = at("y_tanh", [P, T, CONV], X + 12 * kb)
        S = 144 * kb
        W = S + 6 * kb
        xg = at("xg", [P, 2, T, COL], W)
        wide = at("wide", [P, D], W)
        gain = at("gain", [P, D], W + 8 * kb)
        mk_tok = at("mk_tok", [P, T, MEM_HEADS, HEAD], W)
        mkT = at("mkT", [P, MEM_HEADS, SEQ], W + 4 * kb)
        mv_tok = at("mv_tok", [P, T, MEM_HEADS, HEAD], W + 8 * kb)
        mq_tok = at("mq_tok", [P, T, MEM_HEADS, HEAD], W + 12 * kb)
        mem_pT = at("mem_pT", [P, 2, T, SEQ], W + 12 * kb)
        gates = at("gates", [P, 3, T, COL], W)
        merged = at("merged", [P, T, COL], W + 12 * kb)
        cT_hi = at("cT_hi", [P, CONV // P, SEQ], S + 22 * kb, F32R)
        cT_lo = at("cT_lo", [P, CONV // P, SEQ], S + 26 * kb, F32R)
        oT_hi = at("oT_hi", [P, HEADS, SEQ], S + 30 * kb, F32R)
        oT_lo = at("oT_lo", [P, HEADS, SEQ], S + 38 * kb, F32R)
        moT_hi = at("moT_hi", [P, MEM_HEADS, SEQ], S + 46 * kb, F32R)
        moT_lo = at("moT_lo", [P, MEM_HEADS, SEQ], S + 50 * kb, F32R)
        relu = at("relu", [P, 2, T, SEQ], S + 22 * kb)
        index = at("index", [P, T, SEQ], S + 26 * kb)
        hidden = at("hidden", [P, 2, T, COL], S + 22 * kb)
        glu_a = at("glu_a", [P, T, CONV], S + 30 * kb)
        glu_g = at("glu_g", [P, T, CONV], S + 34 * kb)
        uT = at("uT", [P, CONV // P, TAPS - 1 + SEQ], S + 38 * kb)
        conv_acc = at("conv_acc", [P, CONV // P, SEQ], S + 54 * kb)
        glu_b = at("glu_b", [P, 2, CONV], S + 54 * kb)
        squares = at("squares", [P, T, COL], S + 58 * kb)
        tap_rows = at("tap_rows", [TAPS + 1, CONV], S + 58 * kb)
        ikwT = at("ikwT", [IKW, SEQ], S + 60 * kb)
        ikw_tok = at("ikw_tok", [P, T, IKW], S + 22 * kb)
        ik_twice = at("ik_twice", [P, T, 2, IDX_DIM], S + 61 * kb)
        gate_bias = at("gate_bias", [P, 3, COL], S + 54 * kb)
        conv_bias = at("conv_bias", [P, COL], S + 60 * kb)
        rope_tmp = at("rope_tmp", [P, 2, P], S + 62 * kb)
        tapT = at("tapT", [P, CONV // P, TAPS + 1], S + 63 * kb)
        small = [S]

        def keep(name, shape, dt=F32):
            tensor = at(name, shape, small[0], dt)
            n = 4
            for s in shape[1:]:
                n *= s
            small[0] += (n + 31) // 32 * 32
            assert small[0] <= S + 6 * kb
            return tensor

        ident = keep("ident", [P, P])
        ikT = keep("ikT", [P, SEQ])
        head_gain = keep("head_gain", [P, 4, HEAD])
        NF = HALF_A + HALF_I
        pos_i = keep("pos_i", [P, T], I32)
        pos_f = keep("pos_f", [P, T])
        freq = keep("freq", [P, NF])
        turns = keep("turns", [P, T, NF])
        angle = keep("angle", [P, T, NF])
        fold = keep("fold", [P, T, NF])
        sin = keep("sin", [P, T, NF])
        cos = keep("cos", [P, T, NF])
        half_pi = keep("half_pi", [P, 1])
        minus_half = keep("minus_half", [P, 8])
        sq_sum = keep("sq_sum", [P, T, CB])
        mem_sum = keep("mem_sum", [P, T, CB])
        mean_sq = keep("mean_sq", [P, 3, T])
        rstd = keep("rstd", [P, 3, T])
        head_sum = keep("head_sum", [P, 8])
        head_rstd = keep("head_rstd", [P, 8])
        iw = keep("iw", [P, T, IDX_HEADS])
        top8 = keep("top8", [P, T, 8])
        neg_max = keep("neg_max", [P, 3, T])
        p_sum = keep("p_sum", [P, 3, T])
        p_inv = keep("p_inv", [P, 3, T])
        bn = keep("bn", [P, T, 6])
        mean_var = keep("mean_var", [P, T, 2])
        ln_rstd = keep("ln_rstd", [P, T])

        ROWS = [(G_MK, mk_tok[:, :, :, :], MEM_HEADS), (G_MQ, mq_tok[:, :, :, :], MEM_HEADS),
                (G_KV, kv_tok[:, :, :, :], KV_HEADS),
                (G_Q0, q_tok[:, :, 0:4], 4), (G_Q1, q_tok[:, :, 4:8], 4)]

        acc = ctx.enter_context(nc.psum_tensor("acc", [P, 2, T, COL], F32))
        tp = ctx.enter_context(nc.psum_tensor("tp", [P, 2, 4, P], F32))
        sc = ctx.enter_context(nc.psum_tensor("sc", [P, 2, T, SEQ], F32))

        x_park = nc.dram_tensor("x_park", (T, P, D), F32, kind="Internal").ap()

        def sem(name):
            return ctx.enter_context(nc.semaphore(name))

        landed = [sem(f"landed{c}") for c in range(CHUNKS)]
        hi_ready = sem("hi_ready")
        lo_ready = sem("lo_ready")
        unit_done = sem("unit_done")
        acc_free = [sem(f"acc_free{i}") for i in range(2)]
        tp_full = sem("tp_full")
        tp_free = [sem(f"tp_free{i}") for i in range(2)]
        tp_hi = sem("tp_hi")
        sc_full = sem("sc_full")
        sc_free = [sem(f"sc_free{i}") for i in range(2)]
        dve_step = sem("dve_step")
        act_step = sem("act_step")
        pool_step = sem("pool_step")
        ready = sem("ready")
        waited = sem("waited")
        x_in = [sem(f"x_in{b}") for b in range(CB)]
        first_gain = [sem(f"first_gain{b}") for b in range(CB)]
        pos_in = sem("pos_in")
        ikwT_here = sem("ikwT_here")
        gain_in = sem("gain_in")
        mem_in = sem("mem_in")
        front_in = sem("front_in")
        ln_in = sem("ln_in")
        bias_in = sem("bias_in")
        parked = sem("parked")
        x_back = sem("x_back")
        out_done = sem("out_done")
        squared = sem("squared")
        mean_ready = sem("mean_ready")
        rstd_ready = sem("rstd_ready")
        scaled = sem("scaled")
        ik_here = sem("ik_here")
        ik_turned = sem("ik_turned")
        iq_turned = sem("iq_turned")
        relu_ready = sem("relu_ready")
        relu_used = sem("relu_used")
        causal_done = sem("causal_done")
        chosen = sem("chosen")
        glu_here = sem("glu_here")
        glu_tanh = sem("glu_tanh")
        glu_done = sem("glu_done")
        pad_ready = sem("pad_ready")
        conv_start = sem("conv_start")
        conv_done = sem("conv_done")
        conv_rest = sem("conv_rest")
        ln_stat = sem("ln_stat")
        ln_root = sem("ln_root")
        ln_done = sem("ln_done")
        ln_scaled = sem("ln_scaled")
        y_tanh_ready = sem("y_tanh_ready")
        swish_done = sem("swish_done")
        rows_here = sem("rows_here")
        head_mean = sem("head_mean")
        rows_ready = sem("rows_ready")
        logits = sem("logits")
        exps = sem("exps")
        inv_ready = sem("inv_ready")
        probs = sem("probs")
        gate_in = sem("gate_in")
        gate_tanh = sem("gate_tanh")
        bias_used = sem("bias_used")
        merged_ready = sem("merged_ready")
        x_new = sem("x_new")
        hid_relu = sem("hid_relu")
        hid_ready = sem("hid_ready")

        NAMES = ["group", "unit", "acc0", "acc1", "fill", "tp0", "tp1", "tp_hi", "score", "sc0", "sc1",
                 "dve_step", "act_step", "pool_step",
                 "gain_in", "mem_in", "front_in", "ln_in", "bias_in", "parked", "x_back", "squared",
                 "mean_ready", "rstd_ready", "scaled", "ik_here", "ik_turned", "iq_turned",
                 "relu_ready", "relu_used", "causal_done", "chosen", "glu_here", "glu_tanh", "glu_done",
                 "pad_ready", "conv_done", "conv_start", "conv_rest", "ln_stat", "ln_root", "ln_done", "ln_scaled",
                 "y_tanh_ready",
                 "swish_done", "rows_here", "head_mean", "rows_ready", "logits", "exps",
                 "inv_ready", "probs", "gate_in", "gate_tanh", "bias_used", "merged_ready",
                 "x_new", "ikwT_here", "hid_relu", "hid_ready"]

        chunked = {"p": P, "k": 4}
        v_in = w_in.rearrange("l (c k p) n -> l c p k n", **chunked)
        v_mem = w_mem_kv.rearrange("l (c k p) n -> l c p k n", **chunked)
        v_ao = w_attn_o.rearrange("l (c k p) n -> l c p k n", **chunked)
        v_mo = w_mem_o.rearrange("l (c k p) n -> l c p k n", **chunked)
        v_co = w_conv_o.rearrange("l (c k p) n -> l c p k n", **chunked)
        v_out = w_out.rearrange("l (c k p) n -> l c p k n", **chunked)
        v_up = w_up.rearrange("l (c k p) n -> l c p k n", **chunked)
        v_down = w_down.rearrange("l (q c k p) n -> l q c p k n", c=CHUNKS, **chunked)
        v_glu_b = conv_in_b.rearrange("l (i n) -> l i n", i=2)
        v_gb = gate_b.rearrange("l (i n) -> l i n", i=3)
        x_rows = x.rearrange("b (t p) d -> p (b t) d", p=P)
        mem_tokens = mem.rearrange("b (t p) d -> (b t) p d", p=P)
        out_tokens = out.rearrange("b (t p) d -> (b t) p d", p=P)

        def rows(row, parts=P):
            return row.partition_broadcast(parts)

        def over(ap, axis, n):
            shape = list(ap.shape)
            return ap.unsqueeze(axis).broadcast_to(shape[:axis] + [n] + shape[axis:])

        FRONT_SRC = {
            G_IKW: (v_in, IK0, IKW), G_IQ0: (v_in, IQ0, COL), G_IQ1: (v_in, IQ0 + COL, COL),
            G_GLUA: (v_in, GLU0, COL), G_GLUG: (v_in, GLU0 + CONV, COL), G_MK: (v_mem, 0, COL),
            G_MV: (v_mem, COL, COL), G_MQ: (v_in, MQ0, COL), G_KV: (v_in, K0, COL),
            G_Q0: (v_in, Q0, COL), G_Q1: (v_in, Q0 + COL, COL),
        }

        def width_of(g):
            return IKW if g == G_IKW else COL

        block = ctx.enter_context(nc.Block())

        @block.sync
        def _(sp):
            here = Place(["unit"])

            def load(c, source):
                sp.wait_ge(lo_ready, here.next("unit", 2))
                sp.sem_inc(waited, 1)
                sp.dma_start(raw[:, c, :, 0:source.shape[-1]], source).then_inc(landed[c], 16)

            sp.wait_ge(x_in[1], 16)
            with sp.Fori(0, LAYERS) as l, here.loop("layer", l, 0, LAYERS):
                for g in range(FRONT):
                    view, c0, w = FRONT_SRC[g]
                    for c in range(CHUNKS):
                        load(c, view[l, c, :, :, c0:c0 + w])
                with sp.Fori(0, CB) as cb, here.loop("merge", cb, 0, CB):
                    for i in range(3):
                        for c in range(CHUNKS):
                            load(c, v_in[l, c, :, :, bass.ds(GATE0 + i * D + cb * COL, COL)])
                    load(0, v_co[l, 0, :, :, bass.ds(cb * COL, COL)])
                    load(1, v_mo[l, 0, :, :, bass.ds(cb * COL, COL)])
                    load(2, v_ao[l, 0, :, :, bass.ds(cb * COL, COL)])
                    load(3, v_ao[l, 1, :, :, bass.ds(cb * COL, COL)])
                for b in range(CB):
                    for c in range(CHUNKS):
                        load(c, v_out[l, c, :, :, b * COL:(b + 1) * COL])
                with sp.Fori(0, FFN // D) as qu, here.loop("ffn", qu, 0, FFN // D):
                    for b in range(CB):
                        for c in range(CHUNKS):
                            load(c, v_up[l, c, :, :, bass.ds(qu * D + b * COL, COL)])
                    for b in range(CB):
                        for c in range(CHUNKS):
                            load(c, v_down[l, qu, c, :, :, b * COL:(b + 1) * COL])
            sp.wait_ge(x_new, LAYERS * (CB + CB * FFN // D))
            sp.dma_start(out_tokens.rearrange("t p d -> p t d"), x_tok[:, :, :]).then_inc(out_done, 16)
            sp.wait_ge(out_done, 16)

        @block.tensor
        def _(pe):
            here = Place(NAMES)
            pe.sem_inc(unit_done, 4)
            for s in (*acc_free, *tp_free, *sc_free):
                pe.sem_inc(s, 1)
            pe.wait_ge(ready, 1)

            def unit(u, a_hi, a_lo, kts, w, pair, first, last):
                if first:
                    pe.wait_ge(acc_free[pair], here.next(f"acc{pair}"))
                pe.wait_ge(lo_ready, here.next("unit") + 8)
                for dk, kt in enumerate(kts):
                    for t in range(T):
                        o = acc[:, pair, t, 0:w]
                        a1, a2 = a_hi[:, kt, t * P:(t + 1) * P], a_lo[:, kt, t * P:(t + 1) * P]
                        w1, w2 = hi[:, u % 4, dk, 0:w], lo[:, u % 4, dk, 0:w]
                        pe.matmul(o, a1, w1, start=first and dk == 0, stop=False)
                        pe.matmul(o, a1, w2, start=False, stop=False)
                        mm = pe.matmul(o, a2, w1, start=False, stop=last and dk == 1)
                mm.then_inc(unit_done, 1)

            def fill(name, tiles):
                b = here.fill(name)
                pe.wait_ge(tp_free[b], here.now(f"tp{b}"))
                if tiles[0].shape[0] < P:
                    pe.sem_inc(waited, 1)
                for i, tile in enumerate(tiles):
                    k, m = tile.shape
                    mm = pe.transpose(tp[0:m, b, i, 0:k], tile, ident[0:k, 0:k])
                mm.then_inc(tp_full, 1)

            def emptied(*names):
                for name in names:
                    b, value = here.emptied(name)
                    pe.wait_ge(tp_free[b], value)

            def emptied_before(n):
                for i in range(n):
                    b = (here.bank + i) % 2
                    pe.wait_ge(tp_free[b], here.now(f"tp{b}") + 1)

            def norm_fill(b, t):
                if t == 0:
                    pe.wait_ge(scaled, here.next("scaled"))
                fill(("norm", b, t), [xg[:, b % 2, t, k * P:(k + 1) * P] for k in range(4)])

            def norm_fills(m):
                for b, n in enumerate(X_BLOCK_DONE):
                    if m - n + 2 in range(T):
                        norm_fill(b, m - n + 2)

            def ikw_unit(u, first, last):
                if first:
                    pe.wait_ge(sc_free[0], here.next("sc0"))
                pe.wait_ge(lo_ready, here.next("unit") + 8)
                for dk in range(2):
                    kt = 2 * u + dk
                    o = sc[0:IKW, 0, 0, :]
                    w1, w2 = hi[:, u % 4, dk, 0:IKW], lo[:, u % 4, dk, 0:IKW]
                    pe.matmul(o, w1, hT_hi[:, kt], start=first and dk == 0, stop=False)
                    pe.matmul(o, w2, hT_hi[:, kt], start=False, stop=False)
                    mm = pe.matmul(o, w1, hT_lo[:, kt], start=False, stop=last and dk == 1)
                mm.then_inc(unit_done, 1)

            def scores(bank, pairs):
                pe.wait_ge(sc_free[bank], here.next(f"sc{bank}"))
                for t, (a, b) in enumerate(pairs):
                    mm = pe.matmul(sc[:, bank, t, :], a, b, start=(t == 0), stop=(t == T - 1),
                                   skip_group_check=True)
                mm.then_inc(sc_full, 1)

            def head_output(j):
                emptied(("p", j, 0))
                b = here.fill(("o", j, 0))
                pe.wait_ge(tp_free[b], here.now(f"tp{b}"))
                o = tp[:, b, 0:2, :].rearrange("p a d -> p (a d)")
                for kt in range(T):
                    if j < MEM_HEADS:
                        v = mv_tok[:, kt, j]
                    else:
                        v = kv_tok[:, kt, KV_HEADS + (j - MEM_HEADS) // (HEADS // KV_HEADS)]
                    pT = mem_pT if j < MEM_HEADS else attn_pT
                    mm = pe.matmul(o, v, pT[:, j % 2, kt, :], start=(kt == 0), stop=(kt == T - 1))
                mm.then_inc(tp_full, 1)

            def side(n):
                for _, what, i, j in [f for f in FILLS if f[0] == n]:
                    name = (what, i, j)
                    if what == "taps":
                        pe.wait_ge(front_in, here.next("front_in", 16 * FRONT_DMAS))
                        pe.sem_inc(waited, 1)
                        fill(name, [tap_rows[:, c * P:(c + 1) * P] for c in range(CONV // P)])
                    elif what == "norm":
                        norm_fill(i, j)
                    elif what == "ikw":
                        if i == 0:
                            pe.wait_ge(ikwT_here, here.next("ikwT_here"))
                        fill(name, [ikwT[:, i * P:(i + 1) * P]])
                    elif what == "mem":
                        if j == 0:
                            pe.wait_ge(scaled, here.next("scaled"))
                        fill(name, [wide[:, k * P:(k + 1) * P] for k in range(4 * j, 4 * j + 4)])
                    elif what == "ik":
                        pe.wait_ge(ik_turned, here.next("ik_turned"))
                        fill(name, [ik_twice[:, t].rearrange("p a d -> p (a d)") for t in range(T)])
                    elif what == "iq":
                        if j == 0:
                            pe.wait_ge(iq_turned, here.next("iq_turned"))
                        two = iq_tok[:, j].rearrange("p (g a) d -> p g (a d)", a=2)
                        fill(name, [two[:, g] for g in range(4 * i, 4 * i + 4)])
                    elif what == "conv_in":
                        if i == 0:
                            pe.wait_ge(glu_done, here.next("glu_done"))
                        fill(name, [glu_a[:, i, c * P:(c + 1) * P] for c in range(CONV // P)])
                    elif what in ("mk", "mq"):
                        if i == 0:
                            pe.wait_ge(rows_ready, here.next("rows_ready"))
                        fill(name, [(mk_tok if what == "mk" else mq_tok)[:, i, h] for h in range(MEM_HEADS)])
                    elif what == "k":
                        if i == 0:
                            pe.wait_ge(rows_ready, here.next("rows_ready"))
                        fill(name, [kv_tok[:, t, i] for t in range(T)])
                    elif what == "q":
                        if j == 0:
                            pe.wait_ge(rows_ready, here.next("rows_ready"))
                        fill(name, [q_tok[:, j, h] for h in range(4 * i, 4 * i + 4)])
                    elif what == "conv_out":
                        if i == 0:
                            pe.wait_ge(conv_done, here.next("conv_done"))
                            pe.wait_ge(conv_rest, here.next("conv_rest"))
                        fill(name, [conv_acc[:, c, i * P:(i + 1) * P] for c in range(CONV // P)])
                    elif what == "conv_row":
                        if i == 0:
                            pe.wait_ge(swish_done, here.next("swish_done"))
                        fill(name, [y_tok[:, i, c * P:(c + 1) * P] for c in range(CONV // P)])
                    elif what == "p":
                        pe.wait_ge(probs, here.next("probs"))
                        fill(name, [s_buf[:, i % 3, t, k * P:(k + 1) * P] for k in range(T) for t in range(T)])
                    elif what == "o":
                        head_output(i)
                if INDEX_AT <= n < INDEX_AT + IDX_HEADS:
                    j, a = divmod(n - INDEX_AT, 2)
                    if n == INDEX_AT:
                        emptied(("ik", 0, 0), ("iq", 1, 1))
                    half = slice(a * IDX_DIM, (a + 1) * IDX_DIM)
                    scores(a, [(iqT[half, j, t * P:(t + 1) * P], ikT[half, :]) for t in range(T)])
                if n in HEAD_AT:
                    j = HEAD_AT.index(n)
                    h = j - MEM_HEADS
                    if j == 0:
                        emptied(("mk", 1, 0), ("mq", 1, 0))
                    if h == 0:
                        emptied(("k", 1, 0), ("q", 0, 1))
                    if h == 4:
                        emptied(("q", 1, 1))
                    for_head = (mqT[:, j], mkT[:, j]) if h < 0 else (qT[:, h], kT[:, h // 4])
                    scores(j % 2, [(for_head[0][:, t * P:(t + 1) * P], for_head[1]) for t in range(T)])

            def merge(first):
                for m in range(4 * UNITS):
                    if m < 24:
                        g, u = divmod(m, UNITS)
                        unit(u, hT_hi, hT_lo, (2 * u, 2 * u + 1), COL, (1, 0, 1)[g], u == 0,
                             u == UNITS - 1)
                    elif m < 26:
                        if first and m == 24:
                            emptied(("conv_row", 1, 0))
                        u = m - 24
                        unit(m % 8, cT_hi, cT_lo, (2 * u, 2 * u + 1), COL, 0, u == 0, u == 1)
                    elif m < 28:
                        if first and m == 26:
                            emptied(("o", MEM_HEADS - 1, 0))
                        u = m - 26
                        unit(m % 8, moT_hi, moT_lo, (2 * u, 2 * u + 1), COL, 1, u == 0, u == 1)
                    else:
                        u = m - 28
                        if first:
                            emptied(("o", MEM_HEADS + 2 * u + 1, 0))
                        unit(m % 8, oT_hi, oT_lo, (2 * u, 2 * u + 1), COL, 0, u == 0, u == 3)
                    if first:
                        side(FRONT * UNITS + m)
                    else:
                        merged_fill(m - 7)

            def merged_fill(t):
                if t == 0:
                    pe.wait_ge(merged_ready, here.next("merged_ready"))
                if t in range(T):
                    fill(("merged", t), [merged[:, t, k * P:(k + 1) * P] for k in range(4)])

            def mlp(first, last):
                for m in range(8 * UNITS):
                    g, u = divmod(m, UNITS)
                    pair = (1, 0)[g % 2]
                    if first and m == 0:
                        emptied_before(2)
                    if first and m == 6:
                        emptied(("norm", CB - 1, 0), ("norm", CB - 1, 1))
                    if g < CB:
                        unit(u, hT_hi, hT_lo, (2 * u, 2 * u + 1), COL, pair, u == 0, u == UNITS - 1)
                    else:
                        if m == 32:
                            emptied(("hidden", 2, 1))
                        if m == 38:
                            emptied(("hidden", 3, 1))
                        unit(u, bT_hi, bT_lo, (2 * u, 2 * u + 1), COL, pair, u == 0, u == UNITS - 1)
                    b, t = divmod(m - 11, UNITS)
                    if b in range(CB) and t in range(T):
                        if t == 0:
                            pe.wait_ge(hid_ready, here.next("hid_ready"))
                        fill(("hidden", b, t), [hidden[:, b % 2, t, k * P:(k + 1) * P] for k in range(4)])
                    if first and m in NORM_FILL:
                        norm_fill(CB - 1, NORM_FILL.index(m))
                    if last:
                        norm_fills(m - CB * UNITS)

            for b in range(CB - 1):
                for t in range(T):
                    norm_fill(b, t)
            with pe.Fori(0, LAYERS) as l, here.loop("layer", l, 0, LAYERS):
                for n in range(FRONT * UNITS):
                    g, u = divmod(n, UNITS)
                    if n == 0:
                        emptied_before(2)
                    if n == 6:
                        emptied(("norm", CB - 1, 0), ("norm", CB - 1, 1))
                    if g == G_MK and u % 2 == 0:
                        emptied(("mem", 1, u // 2))
                    a = (bT_hi, bT_lo) if g in (G_MK, G_MV) else (hT_hi, hT_lo)
                    if g == G_IKW:
                        ikw_unit(u, u == 0, u == UNITS - 1)
                    else:
                        unit(u, *a, (2 * u, 2 * u + 1), COL, PAIR[g], u == 0, u == UNITS - 1)
                    side(n)
                merge(True)
                with pe.Fori(1, CB) as c, here.loop("merge", c, 1, CB - 1):
                    merge(False)
                for m in range(CB * UNITS):
                    g, u = divmod(m, UNITS)
                    if m == 6:
                        emptied(("merged", 1))
                    unit(u, bT_hi, bT_lo, (2 * u, 2 * u + 1), COL, (1, 0)[g % 2], u == 0, u == UNITS - 1)
                    merged_fill(m - 3)
                    norm_fills(m)
                mlp(True, False)
                with pe.Fori(1, FFN // D - 1) as qu, here.loop("ffn", qu, 1, FFN // D - 2):
                    mlp(False, False)
                mlp(False, True)

        @block.scalar
        def _(act):
            here = Place(NAMES)

            def alone():
                act.sem_inc(waited, 1)

            def split(u, w):
                c = u // 2
                if u % 2 == 0:
                    if u == 0:
                        here.next("group")
                    act.wait_ge(landed[c], here.now("group") * 16)
                act.wait_ge(unit_done, here.next("unit"))
                act.activation(hi[:, u % 4, :, 0:w], raw[:, c, 2 * (u % 2):2 * (u % 2) + 2, 0:w],
                               ACT.Copy).then_inc(hi_ready, 1)

            def take(name, out_ap, n=4, w=P, scale=1.0):
                act.wait_ge(tp_full, here.next("fill"))
                b = here.fill(name)
                act.activation(out_ap, tp[:, b, 0:n, 0:w], ACT.Copy, scale=scale).then_inc(tp_free[b], 1)

            def take_high(name, out_ap, n=4, scale=1.0):
                act.wait_ge(tp_full, here.next("fill"))
                b = here.fill(name)
                act.activation(out_ap, tp[:, b, 0:n, :], ACT.Copy, scale=scale).then_inc(tp_hi, 1)

            def square_sum(source, sums):
                if here.n["squared"] or here.base["squared"].__class__ is not int:
                    act.wait_ge(squared, here.now("squared"))
                here.next("squared")
                act.activation(sc[:, 1].rearrange("p t s -> p (t s)"), source, ACT.Square,
                               accum_out=sums).then_inc(squared, 1)

            def take_norm(b, t):
                take_high(("norm", b, t), hT_hi[:, 4 * b:4 * b + 4, t * P:(t + 1) * P])

            def x_side(m):
                for b, n in enumerate(X_BLOCK_DONE):
                    if m - n == 1:
                        x_squares(b)
                    if m - n - 2 in range(T):
                        take_norm(b, m - n - 2)

            def block_done(e):
                act.wait_ge(unit_done, origin[0] + e + 5)

            def side(n):
                for _, what, i, j in [f for f in FILLS if f[0] + EMPTY_AFTER == n]:
                    name = (what, i, j)
                    cols = slice(i * P, (i + 1) * P)
                    if what == "taps":
                        take(name, tapT[:, :, :], w=TAPS + 1)
                    elif what == "norm":
                        take_norm(i, j)
                    elif what == "ikw":
                        act.wait_ge(tp_full, here.next("fill"))
                        b = here.fill(name)
                        act.activation(ikw_tok[:, i], tp[:, b, 0, 0:IKW], ACT.Copy,
                                       scale=rstd[:, 0, i:i + 1]).then_inc(ik_here, 1)
                        act.wait_ge(ik_here, here.next("ik_here"))
                        act.sem_inc(tp_free[b], 1)
                    elif what == "mem":
                        take_high(name, bT_hi[:, 4 * j:4 * j + 4, cols])
                    elif what == "ik":
                        take(name, ikT[:, :].rearrange("p (t s) -> p t s", t=T), n=2)
                    elif what == "iq":
                        take(name, iqT[:, 4 * i:4 * i + 4, j * P:(j + 1) * P])
                    elif what == "conv_in":
                        if i == 0:
                            act.wait_ge(pad_ready, here.next("pad_ready"))
                        take(name, uT[:, :, TAPS - 1 + i * P:TAPS - 1 + (i + 1) * P], scale=0.5)
                    elif what == "mk":
                        take(name, mkT[:, :, cols])
                    elif what == "mq":
                        take(name, mqT[:, :, cols])
                    elif what == "k":
                        take(name, kT[:, i].rearrange("p (t s) -> p t s", t=T), n=2)
                    elif what == "q":
                        take(name, qT[:, 4 * i:4 * i + 4, j * P:(j + 1) * P])
                    elif what == "conv_out":
                        take(name, y_tok[:, i].rearrange("p (c s) -> p c s", s=P))
                    elif what == "conv_row":
                        take_high(name, cT_hi[:, :, cols], scale=0.5)
                    elif what == "p":
                        pT = mem_pT if i < MEM_HEADS else attn_pT
                        take(name, pT[:, i % 2].rearrange("p k (t s) -> p (k t) s", t=T))
                    elif what == "o":
                        o = moT_hi[:, i] if i < MEM_HEADS else oT_hi[:, i - MEM_HEADS]
                        take_high(name, o.rearrange("p (t s) -> p t s", t=T), n=2)
                if n == X_SQUARES:
                    x_squares(CB - 1)
                if n == IKW_TAKEN:
                    block_done(G_IKW * UNITS + 7)
                    act.activation(ikwT[:, :], sc[0:IKW, 0, 0, :], ACT.Copy).then_inc(ikwT_here, 1)
                    act.wait_ge(ikwT_here, here.next("ikwT_here"))
                    act.sem_inc(sc_free[0], 1)
                for i, g in enumerate((G_IQ0, G_IQ1)):
                    if n == IQ_TAKEN[i]:
                        if i == 0:
                            act.wait_ge(parked, here.next("parked", 32))
                            act.wait_ge(rstd_ready, here.next("rstd_ready"))
                        block_done(g * UNITS + 7)
                        for t in range(T):
                            ins = act.activation(iq_tok[:, t, 8 * i:8 * i + 8, :].rearrange("p h d -> p (h d)"),
                                                 acc[:, PAIR[g], t], ACT.Copy, scale=rstd[:, 0, t:t + 1])
                        ins.then_inc(acc_free[PAIR[g]], 1)
                if n in MEM_SQUARES:
                    act.wait_ge(mem_in, here.next("mem_in", 16))
                    t = MEM_SQUARES.index(n)
                    here.next("scaled")
                    for b in range(CB):
                        square_sum(wide[:, b * COL:(b + 1) * COL], mem_sum[:, t, b:b + 1])
                s = n - INDEX_AT - EMPTY_AFTER
                if s in range(IDX_HEADS):
                    act.wait_ge(sc_full, here.next("score"))
                    if s >= 2:
                        act.wait_ge(relu_used, here.next("relu_used"))
                    act.activation(relu[:, s % 2], sc[:, s % 2], ACT.Relu).then_inc(sc_free[s % 2], 1)
                    if s == IDX_HEADS - 1:
                        here.next("relu_used", 2)
                if n == GLU_TANH:
                    act.wait_ge(glu_here, here.next("glu_here"))
                    act.activation(glu_g[:, :, :], glu_g[:, :, :], ACT.Tanh, scale=0.5).then_inc(glu_tanh, 1)
                if n in ROWS_TAKEN:
                    k = ROWS_TAKEN.index(n)
                    g, dest, heads = ROWS[k]
                    block_done(g * UNITS + 7)
                    kind = 1 if g == G_MK else 0
                    if k == 0:
                        act.wait_ge(rstd_ready, here.next("rstd_ready"))
                    else:
                        act.wait_ge(head_mean, here.next("head_mean"))
                    for t in range(T):
                        act.activation(squares[:, t, 0:heads * HEAD], acc[:, PAIR[g], t, 0:heads * HEAD],
                                       ACT.Square, scale=rstd[:, kind, t:t + 1])
                        ins = act.activation(dest[:, t].rearrange("p h d -> p (h d)"), acc[:, PAIR[g], t],
                                             ACT.Copy, scale=rstd[:, kind, t:t + 1])
                    ins.then_inc(rows_here, 1)
                    act.wait_ge(rows_here, here.next("rows_here"))
                    act.sem_inc(acc_free[PAIR[g]], 1)
                    if k == len(ROWS) - 1:
                        here.next("head_mean")
                if n == MV_TAKEN:
                    block_done(G_MV * UNITS + 7)
                    for t in range(T):
                        ins = act.activation(mv_tok[:, t].rearrange("p h d -> p (h d)"), acc[:, PAIR[G_MV], t],
                                             ACT.Copy, scale=rstd[:, 1, t:t + 1])
                    ins.then_inc(acc_free[PAIR[G_MV]], 1)
                if n - 5 in HEAD_AT:
                    r = HEAD_AT.index(n - 5) % 3
                    act.wait_ge(logits, here.next("logits"))
                    for t in range(T):
                        e = act.activation(s_buf[:, r, t], s_buf[:, r, t], ACT.Exp, bias=neg_max[:, r, t:t + 1],
                                           accum_out=p_sum[:, r, t:t + 1])
                    e.then_inc(exps, 1)
                if n - 6 in HEAD_AT:
                    r = HEAD_AT.index(n - 6) % 3
                    act.wait_ge(inv_ready, here.next("inv_ready"))
                    for t in range(T):
                        e = act.activation(s_buf[:, r, t], s_buf[:, r, t], ACT.Copy, scale=p_inv[:, r, t:t + 1])
                    e.then_inc(probs, 1)
                if n == Y_TANH:
                    act.wait_ge(ln_scaled, here.next("ln_scaled"))
                    act.activation(y_tanh[:, :, :], y_tok[:, :, :], ACT.Tanh, scale=0.5).then_inc(y_tanh_ready, 1)

            def merged_take(t, cols):
                if t in range(T):
                    act.wait_ge(tp_full, here.next("fill"))
                    alone()
                    b = here.fill(("merged", t))
                    act.activation(bT_hi[:, cols, t * P:(t + 1) * P], tp[:, b], ACT.Copy,
                                   scale=0.5).then_inc(tp_hi, 1)

            def merge(first, c):
                for m in range(4 * UNITS):
                    split(m % UNITS, COL)
                    if first:
                        side(FRONT * UNITS + m)
                    else:
                        merged_take(m - 11, bass.ds((c - 1) * 4, 4))
                    if m in GATE_TANH:
                        i = GATE_TANH.index(m)
                        act.wait_ge(gate_in, here.next("gate_in"))
                        act.activation(gates[:, i], gates[:, i], ACT.Tanh, scale=0.5).then_inc(gate_tanh, 1)

            def x_squares(b):
                act.wait_ge(scaled, here.next("scaled"))
                for t in range(T):
                    square_sum(x_tok[:, t, b * COL:(b + 1) * COL], sq_sum[:, t, b:b + 1])

            def mlp(first, last):
                for m in range(8 * UNITS):
                    split(m % UNITS, COL)
                    if first and m == X_SQUARES:
                        x_squares(CB - 1)
                    if first and m - 4 in NORM_FILL:
                        take_norm(CB - 1, NORM_FILL.index(m - 4))
                    b, r = divmod(m - 12, UNITS)
                    if r == 0 and b in range(CB):
                        if first and b == 0:
                            act.wait_ge(rstd_ready, here.next("rstd_ready"))
                        block_done(b * UNITS + 7)
                        for t in range(T):
                            ins = act.activation(hidden[:, b % 2, t], acc[:, (1, 0)[b % 2], t], ACT.Relu,
                                                 scale=rstd[:, 2, t:t + 1])
                        ins.then_inc(hid_relu, 1)
                        act.wait_ge(hid_relu, here.next("hid_relu"))
                        act.sem_inc(acc_free[(1, 0)[b % 2]], 1)
                    b, t = divmod(m - 15, UNITS)
                    if b in range(CB) and t in range(T):
                        take_high(("hidden", b, t), bT_hi[:, 4 * b:4 * b + 4, t * P:(t + 1) * P])
                    if last:
                        x_side(m - CB * UNITS)

            origin = [0]
            for b in range(CB):
                act.dma_start(gain[:, b * COL:(b + 1) * COL],
                              rows(norm1_g[0, b * COL:(b + 1) * COL])).then_inc(first_gain[b], 16)
                act.dma_start(x_tok[:, :, b * COL:(b + 1) * COL],
                              x_rows[:, :, b * COL:(b + 1) * COL]).then_inc(x_in[b], 16)
            act.wait_ge(ready, 4)
            act.activation(sin[:, :, :], angle[:, :, :], ACT.Sin).then_inc(act_step, 1)
            act.activation(cos[:, :, :], fold[:, :, :], ACT.Sin, scale=-1.0,
                           bias=half_pi[:, 0:1]).then_inc(act_step, 1)
            here.next("act_step", 2)
            for b in range(CB - 1):
                x_squares(b)
                for t in range(T):
                    take_norm(b, t)
            with act.Fori(0, LAYERS) as l, here.loop("layer", l, 0, LAYERS):
                origin[0] = here.now("unit")
                for n in range(FRONT * UNITS):
                    split(n % UNITS, width_of(n // UNITS))
                    side(n)
                merge(True, 0)
                with act.Fori(1, CB) as c, here.loop("merge", c, 1, CB - 1):
                    merge(False, c)
                for m in range(CB * UNITS):
                    split(m % UNITS, COL)
                    merged_take(m - 7, slice(KT - 4, KT))
                    x_side(m)
                here.next("score", MEM_HEADS + HEADS)
                origin[0] = here.now("unit")
                mlp(True, False)
                with act.Fori(1, FFN // D - 1) as qu, here.loop("ffn", qu, 1, FFN // D - 2):
                    origin[0] = here.now("unit")
                    mlp(False, False)
                origin[0] = here.now("unit")
                mlp(False, True)

        @block.vector
        def _(dve):
            here = Place(NAMES)
            origin = [0]

            def step(ins):
                ins.then_inc(dve_step, 1)
                here.next("dve_step")

            def settle(back=0):
                dve.wait_ge(dve_step, here.now("dve_step") - back)

            def link(ins):
                step(ins)
                settle()

            def alone():
                dve.sem_inc(waited, 1)

            def split(u, w):
                dve.wait_ge(hi_ready, here.next("unit"))
                dve.tensor_tensor(lo[:, u % 4, :, 0:w], raw[:, u // 2, 2 * (u % 2):2 * (u % 2) + 2, 0:w],
                                  hi[:, u % 4, :, 0:w].bitcast(F32), ALU.subtract).then_inc(lo_ready, 1)

            def take_low(name, dst, src, n=4, scale=None):
                b = here.fill(name)
                dve.wait_ge(tp_hi, here.next("tp_hi"))
                if scale is None:
                    ins = dve.tensor_tensor(dst, tp[:, b, 0:n, :], src.bitcast(F32), ALU.subtract)
                else:
                    ins = dve.scalar_tensor_tensor(dst, tp[:, b, 0:n, :], scale, src.bitcast(F32), ALU.mult,
                                                   ALU.subtract)
                ins.then_inc(tp_free[b], 1)

            def means(kind, sums):
                dve.wait_ge(squared, here.next("squared", T * CB))
                link(dve.tensor_reduce(mean_sq[:, kind], sums[:, :, :], AX_X, ALU.add))
                dve.tensor_scalar(mean_sq[:, kind], mean_sq[:, kind], 1.0 / D, EPS, ALU.mult,
                                  ALU.add).then_inc(mean_ready, 1)

            def take_norm(b, t):
                here.next("fill")
                kts, cols = slice(4 * b, 4 * b + 4), slice(t * P, (t + 1) * P)
                take_low(("norm", b, t), hT_lo[:, kts, cols], hT_hi[:, kts, cols])

            def scale_block(b):
                cols = slice(b * COL, (b + 1) * COL)
                dve.tensor_tensor(xg[:, b % 2], x_tok[:, :, cols], over(gain[:, cols], 1, T),
                                  ALU.mult).then_inc(scaled, 1)

            def x_side(m):
                for b, n in enumerate(X_BLOCK_DONE):
                    if m == n:
                        if b == 0:
                            dve.wait_ge(gain_in, here.next("gain_in", 16))
                        scale_block(b)
                    if m - n - 2 in range(T):
                        take_norm(b, m - n - 2)

            def block_done(e):
                dve.wait_ge(unit_done, origin[0] + e + 5)

            def conv_steps(n):
                done = sum(count for at_, count in DVE_CONV if at_ < n)
                for i in range(done, min(done + dict(DVE_CONV).get(n, 0), TAPS * DVE_TILES)):
                    k, c = divmod(i, DVE_TILES)
                    if i == 0:
                        for name in (("taps", 0, 0), ("conv_in", 1, 0)):
                            b, value = here.emptied(name)
                            dve.wait_ge(tp_free[b], value)
                        dve.sem_inc(conv_start, 1)
                    src = uT[:, c, k:k + SEQ]
                    if k == 0:
                        step(dve.tensor_scalar(conv_acc[:, c], src, tapT[:, c, 0:1], tapT[:, c, TAPS:TAPS + 1],
                                               ALU.mult, ALU.add))
                    else:
                        settle(DVE_TILES - 1)
                        step(dve.scalar_tensor_tensor(conv_acc[:, c], src, tapT[:, c, k:k + 1], conv_acc[:, c],
                                                      ALU.mult, ALU.add))
                    if i == TAPS * DVE_TILES - 1:
                        settle()
                        dve.sem_inc(conv_done, 1)

            def select_round(r):
                if r == 0:
                    dve.wait_ge(causal_done, here.next("causal_done"))
                    alone()
                for t in range(T):
                    keys = (t + 1) * P
                    step(dve.max(top8[:, t], index[:, t, 0:keys]))
                for t in range(T):
                    keys = (t + 1) * P
                    settle(1 if t == 0 else 1)
                    alone()
                    step(dve.match_replace(index[:, t, 0:keys], top8[:, t], index[:, t, 0:keys], TAKEN))
                settle()
                alone()

            def head(j):
                r = j % 3
                dve.wait_ge(sc_full, here.next("score"))
                if j >= 3:
                    dve.wait_ge(tp_full, here.base["fill"] + fills_until(("p", j - 3, 0)))
                if j < MEM_HEADS:
                    ins = dve.tensor_scalar(s_buf[:, r], sc[:, j % 2], SCALE, None, ALU.mult)
                else:
                    if j == MEM_HEADS:
                        dve.wait_ge(causal_done, here.next("causal_done"))
                    ins = dve.scalar_tensor_tensor(s_buf[:, r], sc[:, j % 2], SCALE, mask[:, :, :], ALU.mult,
                                                   ALU.add)
                ins.then_inc(sc_free[j % 2], 1)
                here.next(f"sc{j % 2}")
                dve.wait_ge(sc_free[j % 2], here.now(f"sc{j % 2}") + 1)
                dve.tensor_reduce(neg_max[:, r], s_buf[:, r], AX_X, ALU.max, negate=True).then_inc(logits, 1)

            def side(n):
                for _, what, i, j in [f for f in FILLS if f[0] + EMPTY_AFTER == n]:
                    name = (what, i, j)
                    if what == "norm":
                        take_norm(i, j)
                        continue
                    here.next("fill")
                    cols = slice(i * P, (i + 1) * P)
                    if what == "mem":
                        take_low(name, bT_lo[:, 4 * j:4 * j + 4, cols], bT_hi[:, 4 * j:4 * j + 4, cols])
                    elif what == "conv_row":
                        take_low(name, cT_lo[:, :, cols], cT_hi[:, :, cols], scale=0.5)
                    elif what == "o":
                        h, l_ = (moT_hi[:, i], moT_lo[:, i]) if i < MEM_HEADS else \
                            (oT_hi[:, i - MEM_HEADS], oT_lo[:, i - MEM_HEADS])
                        take_low(name, l_.rearrange("p (t s) -> p t s", t=T),
                                 h.rearrange("p (t s) -> p t s", t=T), n=2)
                    else:
                        here.fill(name)
                if n == X_MEAN:
                    means(0, sq_sum)
                if n in MEM_SCALED:
                    if n == MEM_SCALED[0]:
                        dve.wait_ge(gain_in, here.next("gain_in", 16))
                    dve.wait_ge(squared, here.now("squared") + CB * (MEM_SCALED.index(n) + 1))
                    dve.tensor_tensor(wide[:, :], wide[:, :], gain[:, :], ALU.mult).then_inc(scaled, 1)
                if n == MEM_MEAN:
                    means(1, mem_sum)
                if n - INDEX_AT - EMPTY_AFTER in range(IDX_HEADS):
                    s = n - INDEX_AT - EMPTY_AFTER
                    if s == 0:
                        here.next("sc0")
                        dve.wait_ge(ik_turned, here.next("ik_turned"))
                    here.next(f"sc{s % 2}")
                    dve.wait_ge(sc_free[s % 2], here.now(f"sc{s % 2}") + 1)
                    for t in range(T):
                        w = iw[:, t, s:s + 1]
                        if s == 0:
                            ins = dve.tensor_scalar(index[:, t], relu[:, 0, t], w, None, ALU.mult)
                        else:
                            ins = dve.scalar_tensor_tensor(index[:, t], relu[:, s % 2, t], w, index[:, t],
                                                           ALU.mult, ALU.add)
                    ins.then_inc(relu_used, 1)
                    dve.wait_ge(relu_used, here.next("relu_used"))
                    here.next("score")
                if n == GLU_A_TAKEN:
                    dve.wait_ge(front_in, here.next("front_in", 16 * FRONT_DMAS))
                    dve.wait_ge(rstd_ready, here.next("rstd_ready"))
                    block_done(G_GLUA * UNITS + 7)
                    for t in range(T):
                        ins = dve.scalar_tensor_tensor(glu_a[:, t], acc[:, PAIR[G_GLUA], t], rstd[:, 0, t:t + 1],
                                                       glu_b[:, 0], ALU.mult, ALU.add)
                    ins.then_inc(acc_free[PAIR[G_GLUA]], 1)
                if n == GLU_G_TAKEN:
                    block_done(G_GLUG * UNITS + 7)
                    for t in range(T):
                        ins = dve.scalar_tensor_tensor(glu_g[:, t], acc[:, PAIR[G_GLUG], t], rstd[:, 0, t:t + 1],
                                                       glu_b[:, 1], ALU.mult, ALU.add)
                    ins.then_inc(glu_here, 1)
                    dve.wait_ge(glu_here, here.next("glu_here"))
                    dve.sem_inc(acc_free[PAIR[G_GLUG]], 1)
                if n == GLU_TANH + 1:
                    dve.wait_ge(glu_tanh, here.next("glu_tanh"))
                    dve.scalar_tensor_tensor(glu_a[:, :, :], glu_g[:, :, :], 1.0, glu_a[:, :, :], ALU.add,
                                             ALU.mult).then_inc(glu_done, 1)
                conv_steps(n)
                r, rest = divmod(n - TOPK_AT, 3)
                if rest == 0 and r in range(TOPK // 8):
                    select_round(r)
                if rest == 1 and r == TOPK // 8 - 1:
                    dve.tensor_scalar(mask[:, :, :], index[:, :, :], TAKEN, -BIG, ALU.not_equal,
                                      ALU.mult).then_inc(chosen, 1)
                if n - 1 in ROWS_TAKEN:
                    k = ROWS_TAKEN.index(n - 1)
                    _, dest, heads = ROWS[k]
                    dve.wait_ge(rows_here, here.next("rows_here"))
                    if k > 0:
                        dve.wait_ge(rows_ready, here.next("rows_ready"))
                    link(dve.tensor_reduce(head_sum[:, 0:T * heads].rearrange("p (t h) -> p t h", t=T),
                                           squares[:, :, 0:heads * HEAD].rearrange("p t (h d) -> p t h d", d=HEAD),
                                           AX_X, ALU.add))
                    dve.tensor_scalar(head_sum[:, 0:T * heads], head_sum[:, 0:T * heads], 1.0 / HEAD, EPS,
                                      ALU.mult, ALU.add).then_inc(head_mean, 1)
                    if k == len(ROWS) - 1:
                        here.next("rows_ready")
                if n - 4 in HEAD_AT:
                    head(HEAD_AT.index(n - 4))
                if n - 6 in HEAD_AT:
                    r = HEAD_AT.index(n - 6) % 3
                    dve.wait_ge(exps, here.next("exps"))
                    dve.reciprocal(p_inv[:, r], p_sum[:, r]).then_inc(inv_ready, 1)
                if n == LN_STATS:
                    b, value = here.emptied(("conv_out", 1, 0))
                    dve.wait_ge(tp_free[b], value)
                    for t in range(T):
                        step(dve.bn_stats(bn[:, t], y_tok[:, t]))
                    settle()
                    alone()
                    for t in range(T):
                        step(dve.bn_aggr(mean_var[:, t], bn[:, t]))
                    settle()
                    dve.tensor_scalar(ln_rstd[:, :], mean_var[:, :, 1], EPS, None, ALU.add).then_inc(ln_stat, 1)
                if n == LN_APPLY:
                    dve.wait_ge(ln_root, here.next("ln_root"))
                    for t in range(T):
                        ins = dve.tensor_scalar(y_tok[:, t], y_tok[:, t], mean_var[:, t, 0:1], ln_rstd[:, t:t + 1],
                                                ALU.subtract, ALU.mult)
                    ins.then_inc(ln_done, 1)
                if n == Y_TANH + 1:
                    dve.wait_ge(y_tanh_ready, here.next("y_tanh_ready"))
                    dve.scalar_tensor_tensor(y_tok[:, :, :], y_tanh[:, :, :], 1.0, y_tok[:, :, :], ALU.add,
                                             ALU.mult).then_inc(swish_done, 1)

            def attention_merge(e):
                block_done(e)
                link(dve.scalar_tensor_tensor(gates[:, 0], gates[:, 0], 1.0, acc[:, 0], ALU.add, ALU.mult))
                dve.sem_inc(acc_free[0], 1)
                dve.tensor_tensor(merged[:, :, :], merged[:, :, :], gates[:, 0], ALU.add).then_inc(merged_ready, 1)

            def merged_low(t, cols):
                if t in range(T):
                    c = slice(t * P, (t + 1) * P)
                    here.next("fill")
                    take_low(("merged", t), bT_lo[:, cols, c], bT_hi[:, cols, c], scale=0.5)

            def merge(first, c):
                for m in range(4 * UNITS):
                    split(m % UNITS, COL)
                    if first:
                        side(FRONT * UNITS + m)
                    else:
                        merged_low(m - 11, bass.ds((c - 1) * 4, 4))
                        if m == 4:
                            attention_merge(-1)
                    start = FRONT * UNITS if first else 0
                    if m in GATE_TAKEN:
                        i = GATE_TAKEN.index(m)
                        if i == 0:
                            dve.wait_ge(bias_in, here.next("bias_in", 32))
                        block_done(start + 8 * i + 7)
                        for t in range(T):
                            ins = dve.scalar_tensor_tensor(gates[:, i, t], acc[:, (1, 0, 1)[i], t],
                                                           rstd[:, 0, t:t + 1], gate_bias[:, i], ALU.mult, ALU.add)
                        ins.then_inc(gate_in, 1)
                        dve.wait_ge(gate_in, here.next("gate_in"))
                        dve.sem_inc(acc_free[(1, 0, 1)[i]], 1)
                    if m == 29:
                        block_done(start + 25)
                        dve.tensor_tensor(merged[:, :, :], acc[:, 0], over(conv_bias[:, :], 1, T),
                                          ALU.add).then_inc(bias_used, 1)
                        dve.wait_ge(bias_used, here.next("bias_used"))
                        dve.sem_inc(acc_free[0], 1)
                    if m == 31:
                        dve.wait_ge(gate_tanh, here.next("gate_tanh", 3))
                        block_done(start + 27)
                        link(dve.scalar_tensor_tensor(gates[:, 1], gates[:, 1], 1.0, acc[:, 1], ALU.add, ALU.mult))
                        dve.sem_inc(acc_free[1], 1)
                    if m == 31:
                        link(dve.scalar_tensor_tensor(merged[:, :, :], gates[:, 2], 1.0, merged[:, :, :], ALU.add,
                                                      ALU.mult))
                        link(dve.tensor_tensor(merged[:, :, :], merged[:, :, :], gates[:, 1], ALU.add))

            def add_block(b, pair, e):
                block_done(e)
                xb = x_tok[:, :, b * COL:(b + 1) * COL]
                dve.tensor_tensor(xb, acc[:, pair], xb, ALU.add).then_inc(x_new, 1)
                dve.wait_ge(x_new, here.next("x_new"))
                dve.sem_inc(acc_free[pair], 1)

            def mlp(first, last):
                for m in range(8 * UNITS):
                    split(m % UNITS, COL)
                    if m == 3:
                        add_block(CB - 1, 0, -1)
                        if first:
                            scale_block(CB - 1)
                    if first and m == X_MEAN:
                        means(2, sq_sum)
                    if first and m - 4 in NORM_FILL:
                        take_norm(CB - 1, NORM_FILL.index(m - 4))
                    b, r = divmod(m - 13, UNITS)
                    if r == 0 and b in range(CB):
                        dve.wait_ge(hid_relu, here.next("hid_relu"))
                        dve.tensor_tensor(hidden[:, b % 2], hidden[:, b % 2], hidden[:, b % 2],
                                          ALU.mult).then_inc(hid_ready, 1)
                    b, t = divmod(m - 15, UNITS)
                    if b in range(CB) and t in range(T):
                        here.next("fill")
                        kts, cols = slice(4 * b, 4 * b + 4), slice(t * P, (t + 1) * P)
                        take_low(("hidden", b, t), bT_lo[:, kts, cols], bT_hi[:, kts, cols])
                    if m - CB * UNITS in X_BLOCK_DONE:
                        b = X_BLOCK_DONE.index(m - CB * UNITS)
                        add_block(b, (1, 0)[b % 2], 8 * b + 39)
                    if last:
                        x_side(m - CB * UNITS)

            dve.sem_inc(lo_ready, 8)
            dve.wait_ge(pos_in, 16)
            dve.wait_ge(ready, 3)
            link(dve.tensor_copy(pos_f[:, :], pos_i[:, :]))
            for t in range(T):
                step(dve.tensor_scalar(angle[:, t], freq[:, :], pos_f[:, t:t + 1], None, ALU.mult))
            settle()
            link(dve.tensor_scalar(turns[:, :, :], angle[:, :, :], 1.0 / TWO_PI, ROUND, ALU.mult, ALU.add))
            link(dve.tensor_scalar(turns[:, :, :], turns[:, :, :], ROUND, None, ALU.subtract))
            for part in (PI_1, PI_2, PI_3):
                link(dve.scalar_tensor_tensor(angle[:, :, :], turns[:, :, :], -part, angle[:, :, :],
                                              ALU.mult, ALU.add))
            link(dve.tensor_scalar(angle[:, :, :], angle[:, :, :], PI_MAX, -PI_MAX, ALU.min, ALU.max))
            dve.scalar_tensor_tensor(fold[:, :, :], angle[:, :, :], -1.0, angle[:, :, :], ALU.mult,
                                     ALU.max).then_inc(ready, 1)
            for b in range(CB):
                dve.wait_ge(first_gain[b], 16)
                dve.wait_ge(x_in[b], 16)
                if b >= 2:
                    dve.wait_ge(tp_full, T * (b - 1))
                if b < CB - 1:
                    scale_block(b)
                if b >= 1:
                    for t in range(T):
                        take_norm(b - 1, t)
            with dve.Fori(0, LAYERS) as l, here.loop("layer", l, 0, LAYERS):
                origin[0] = here.now("unit")
                for n in range(FRONT * UNITS):
                    split(n % UNITS, width_of(n // UNITS))
                    if n == 0:
                        scale_block(CB - 1)
                    side(n)
                merge(True, 0)
                alone()
                with dve.Fori(1, CB) as c, here.loop("merge", c, 1, CB - 1):
                    origin[0] = here.now("unit")
                    merge(False, c)
                origin[0] = here.now("unit")
                for m in range(CB * UNITS):
                    split(m % UNITS, COL)
                    merged_low(m - 7, slice(KT - 4, KT))
                    if m == 4:
                        attention_merge(-1)
                    if m in X_BLOCK_DONE:
                        b = X_BLOCK_DONE.index(m)
                        if b == 0:
                            dve.wait_ge(x_back, here.next("x_back", 16))
                        add_block(b, (1, 0)[b % 2], 8 * b + 7)
                    x_side(m)
                origin[0] = here.now("unit")
                mlp(True, False)
                with dve.Fori(1, FFN // D - 1) as qu, here.loop("ffn", qu, 1, FFN // D - 2):
                    origin[0] = here.now("unit")
                    mlp(False, False)
                origin[0] = here.now("unit")
                mlp(False, True)
                origin[0] = here.now("unit")
                add_block(CB - 1, 0, -1)
                here.next("rstd_ready", 2)

        @block.gpsimd
        def _(pool):
            here = Place(NAMES)

            def link(ins):
                ins.then_inc(pool_step, 1)
                pool.wait_ge(pool_step, here.next("pool_step"))
                alone()

            def alone():
                pool.sem_inc(waited, 1)

            def rotate(rows_, half, f0):
                heads = rows_.shape[2]
                a, b = rows_[:, :, :, 0:half], rows_[:, :, :, half:2 * half]
                cs, sn = (over(tab[:, :, f0:f0 + half], 2, heads) for tab in (cos, sin))
                bs, as_ = (rope_tmp[:, i, 0:T * heads * half].rearrange("p (t h d) -> p t h d", t=T, h=heads)
                           for i in range(2))
                link(pool.tensor_tensor(bs, b, sn, ALU.mult))
                link(pool.tensor_tensor(as_, a, sn, ALU.mult))
                link(pool.tensor_tensor(a, a, cs, ALU.mult))
                link(pool.tensor_tensor(b, b, cs, ALU.mult))
                link(pool.tensor_tensor(a, a, bs, ALU.subtract))
                return pool.tensor_tensor(b, b, as_, ALU.add)

            def root(kind):
                pool.wait_ge(mean_ready, here.next("mean_ready"))
                pool.tensor_tensor(rstd[:, kind], mean_sq[:, kind], minus_half[:, 0:T],
                                   ALU.pow).then_inc(rstd_ready, 1)

            def side(n, l):
                if n == MEM_LOAD + EMPTY_AFTER:
                    pool.wait_ge(unit_done, here.now("unit") + 5 + MEM_LOAD)
                    alone()
                    pool.wait_ge(scaled, here.next("scaled"))
                    alone()
                    pool.dma_start(gain[:, :], rows(mem_norm_g[l])).then_inc(gain_in, 16)
                    pool.wait_ge(tp_full, here.now("fill") + fills_until(("norm", CB - 1, T - 1)))
                    alone()
                    pool.dma_start(wide[:, :], mem_tokens[0]).then_inc(mem_in, 16)
                    pool.dma_start(tap_rows[0:TAPS, :], conv_w[l]).then_inc(front_in, 16)
                    pool.dma_start(tap_rows[TAPS:TAPS + 1, :], conv_b[l].unsqueeze(0)).then_inc(front_in, 16)
                    pool.dma_start(glu_b[:, :, :], rows(v_glu_b[l])).then_inc(front_in, 16)
                    for i, g in enumerate((q_norm_g, k_norm_g, mq_norm_g, mk_norm_g)):
                        pool.dma_start(head_gain[:, i], rows(g[l])).then_inc(front_in, 16)
                if n == MEM_MEAN + 1:
                    root(1)
                if n == IKW_FILL[-1] + EMPTY_AFTER:
                    pool.wait_ge(ik_here, here.next("ik_here", T))
                    alone()
                    link(pool.tensor_scalar(iw[:, :, :], ikw_tok[:, :, IDX_DIM:IKW], IDX_SCALE, None, ALU.mult))
                    link(rotate(ikw_tok[:, :, 0:IDX_DIM].unsqueeze(2), HALF_I, HALF_A))
                    pool.tensor_copy(ik_twice[:, :, :, :], over(ikw_tok[:, :, 0:IDX_DIM], 2, 2)
                                     ).then_inc(ik_turned, 1)
                if n == MEM_FILL[0][-1] + 1:
                    pool.wait_ge(tp_full, here.now("fill") + fills_until(("mem", 0, KT // 4 - 1)))
                    alone()
                    pool.dma_start(wide[:, :], mem_tokens[1]).then_inc(mem_in, 16)
                if n in IQ_TAKEN:
                    i = IQ_TAKEN.index(n)
                    pair = PAIR[(G_IQ0, G_IQ1)[i]]
                    pool.wait_ge(acc_free[pair], here.now(f"acc{pair}") + 2)
                    alone()
                    rotate(iq_tok[:, :, 8 * i:8 * i + 8], HALF_I, HALF_A).then_inc(iq_turned, 1)
                if n - 1 in ROWS_TAKEN:
                    k = ROWS_TAKEN.index(n - 1)
                    _, dest, heads = ROWS[k]
                    dest = dest[:, :, 0:heads]
                    if k == 0:
                        pool.wait_ge(front_in, here.next("front_in", 16 * FRONT_DMAS))
                    pool.wait_ge(head_mean, here.next("head_mean"))
                    link(pool.tensor_tensor(head_rstd[:, 0:T * heads], head_sum[:, 0:T * heads],
                                            minus_half[:, 0:T * heads], ALU.pow))
                    link(pool.tensor_tensor(dest, dest, over(head_rstd[:, 0:T * heads].rearrange(
                        "p (t h) -> p t h", t=T), 3, HEAD), ALU.mult))
                    g = over(over(head_gain[:, (3, 2, 1, 0, 0)[k]], 1, heads), 1, T)
                    ins = pool.tensor_tensor(dest, dest, g, ALU.mult)
                    if k >= 2:
                        link(ins)
                        ins = rotate(dest, HALF_A, 0)
                    ins.then_inc(rows_ready, 1)
                if n == INDEX_AT + EMPTY_AFTER + IDX_HEADS - 1:
                    pool.wait_ge(relu_used, here.next("relu_used", IDX_HEADS))
                    alone()
                    pool.affine_select(out=index[:, :, :], in_=index[:, :, :], pattern=[[P, T], [-1, SEQ]],
                                       compare_op=ALU.is_ge, fill=UNSEEN, base=0,
                                       channel_multiplier=1).then_inc(causal_done, 1)
                if n == TOPK_AT + 3 * (TOPK // 8 - 1) + 1:
                    pool.wait_ge(chosen, here.next("chosen"))
                    alone()
                    pool.affine_select(out=mask[:, :, :], in_=mask[:, :, :], pattern=[[P, T], [-1, SEQ]],
                                       compare_op=ALU.is_ge, fill=-BIG, base=0,
                                       channel_multiplier=1).then_inc(causal_done, 1)
                if n == MASK_FREE:
                    pool.wait_ge(relu_used, here.now("relu_used"))
                    alone()
                    pool.dma_start(ln_g[:, :], rows(conv_ln_g[l])).then_inc(ln_in, 16)
                    pool.dma_start(ln_b[:, :], rows(conv_ln_b[l])).then_inc(ln_in, 16)
                k = n - CONV_AT
                if k in range(TAPS):
                    c = DVE_TILES
                    if k == 0:
                        pool.wait_ge(conv_start, here.next("conv_start"))
                        alone()
                        link(pool.tensor_scalar(conv_acc[:, c], uT[:, c, 0:SEQ], tapT[:, c, 0:1],
                                                tapT[:, c, TAPS:TAPS + 1], ALU.mult, ALU.add))
                    else:
                        link(pool.tensor_scalar(tap_part[:, :], uT[:, c, k:k + SEQ], tapT[:, c, k:k + 1], None,
                                                ALU.mult))
                        ins = pool.tensor_tensor(conv_acc[:, c], conv_acc[:, c], tap_part[:, :], ALU.add)
                        if k < TAPS - 1:
                            link(ins)
                        else:
                            ins.then_inc(conv_rest, 1)
                if n == LN_STATS:
                    pool.wait_ge(ln_stat, here.next("ln_stat"))
                    pool.tensor_tensor(ln_rstd[:, :], ln_rstd[:, :], minus_half[:, 0:T], ALU.pow
                                       ).then_inc(ln_root, 1)
                if n == LN_APPLY:
                    pool.wait_ge(ln_in, here.next("ln_in", 32))
                    pool.wait_ge(ln_done, here.next("ln_done"))
                    link(pool.tensor_tensor(y_tok[:, :, :], y_tok[:, :, :], over(ln_g[:, :], 1, T), ALU.mult))
                    pool.tensor_tensor(y_tok[:, :, :], y_tok[:, :, :], over(ln_b[:, :], 1, T),
                                       ALU.add).then_inc(ln_scaled, 1)

            def biases(l, c):
                alone()
                pool.dma_start(gate_bias[:, :, :], rows(v_gb[l, :, bass.ds(c, COL)])).then_inc(bias_in, 16)
                pool.dma_start(conv_bias[:, :], rows(conv_o_b[l, bass.ds(c, COL)])).then_inc(bias_in, 16)

            pool.dma_start(pos_i[:, :], positions.rearrange("b (t p) -> p (b t)", p=P),
                           allow_slow_non_contiguous=True).then_inc(pos_in, 16)
            link0 = pool.memset(ident[:, :], 0.0)
            link0.then_inc(pool_step, 1)
            here.next("pool_step")
            pool.wait_ge(pool_step, 1)
            pool.affine_select(out=ident[:, :], in_=ident[:, :], compare_op=ALU.not_equal, fill=1.0, base=0,
                               pattern=[[-1, P]], channel_multiplier=1).then_inc(ready, 1)
            for i in range(HALF_A):
                pool.memset(freq[:, i:i + 1], FREQ_A[i])
            for i in range(HALF_I):
                pool.memset(freq[:, HALF_A + i:HALF_A + i + 1], FREQ_I[i])
            pool.memset(half_pi[:, :], TWO_PI / 4).then_inc(ready, 1)
            pool.memset(minus_half[:, :], -0.5).then_inc(ready, 1)
            pool.wait_ge(act_step, 2)
            for b in range(CB):
                pool.wait_ge(x_in[b], 16)
            here.next("fill", T * (CB - 1))
            here.next("scaled", CB - 1)

            with pool.Fori(0, LAYERS) as l, here.loop("layer", l, 0, LAYERS):
                pool.wait_ge(squared, here.now("squared") + T * CB)
                alone()
                for t in range(T):
                    pool.dma_start(x_park[t], x_tok[:, t]).then_inc(parked, 16)
                pool.memset(uT[:, :, 0:TAPS - 1], 0.0).then_inc(pad_ready, 1)
                root(0)
                for n in range(FRONT * UNITS):
                    side(n, l)
                for m in range(4 * UNITS):
                    side(FRONT * UNITS + m, l)
                    if m == BIAS_AT:
                        pool.wait_ge(rows_ready, here.next("rows_ready", len(ROWS)))
                        pool.wait_ge(tp_full, here.now("fill") + fills_until(("conv_out", T - 1, 0)))
                        biases(l, 0)
                with pool.Fori(1, CB) as c, here.loop("merge", c, 1, CB - 1):
                    pool.wait_ge(bias_used, here.next("bias_used"))
                    biases(l, c * COL)
                    here.next("fill", T)
                here.next("bias_used")
                pool.wait_ge(parked, here.next("parked", 32))
                pool.wait_ge(swish_done, here.next("swish_done"))
                alone()
                pool.dma_start(x_tok[:, :, :], x_park.rearrange("t p d -> p t d")).then_inc(x_back, 16)
                pool.wait_ge(tp_full, here.next("fill", len(FILLS) + T))
                alone()
                pool.dma_start(gain[:, :], rows(norm2_g[l])).then_inc(gain_in, 16)
                root(2)
                here.next("fill", T * CB + T * CB * FFN // D + T * (CB - 1))
                pool.wait_ge(scaled, here.next("scaled", T + CB))
                alone()
                pool.dma_start(gain[:, :], rows(norm1_g[LAYERS - 1 - l])).then_inc(gain_in, 16)
                here.next("scaled", CB - 1)
            pool.wait_ge(gain_in, here.now("gain_in"))


INPUTS = ["x", "mem", "positions", "norm1_g", "w_in", "q_norm_g", "k_norm_g", "mem_norm_g", "w_mem_kv", "mq_norm_g",
          "mk_norm_g", "conv_in_b", "conv_w", "conv_b", "conv_ln_g", "conv_ln_b", "gate_b", "w_attn_o", "w_mem_o",
          "w_conv_o", "conv_o_b", "w_out", "norm2_g", "w_up", "w_down"]


def kernel(**inputs):
    import numpy as _np
    import concourse.bacc as _bacc
    from concourse import mybir as _mybir
    from concourse.bass_utils import run_bass_kernel_spmd as _run

    nc = _bacc.Bacc("TRN2", target_bir_lowering=False, num_devices=1)
    arrays, args = {}, []
    for name in INPUTS:
        a = _np.ascontiguousarray(inputs[name])
        arrays[f"in_{name}"] = a
        args.append(nc.dram_tensor(f"in_{name}", a.shape, _mybir.dt.from_np(a.dtype), kind="ExternalInput").ap())
    out = nc.dram_tensor("out", (1, SEQ, D), _mybir.dt.from_np(_np.dtype("float32")), kind="ExternalOutput").ap()
    build(nc, *args, out)
    r = _run(nc, [arrays], core_ids=[0])
    return r.results[0]["out"]
```
